# Optimizing a Trainium2 kernel written in Bass

```python
import jax, jax.numpy as jnp
from jax import lax
import numpy as np

D_MODEL = 1024
BATCH = 1
SEQ = 512
DEPTH = 1
DEC_BATCH = 8
DEC_SEQ = 4
PAST_LEN = 1024
PAGE_SIZE = 128

HEAD_DIM = 64
N_HEADS = 8
KV_HEADS = 2
HPG = N_HEADS // KV_HEADS
ATTN_WIDTH = N_HEADS * HEAD_DIM
KV_WIDTH = KV_HEADS * HEAD_DIM
ROT_DIM = HEAD_DIM // 4
ROT_HALF = ROT_DIM // 2
ROPE_THETA = 500000.0
CMP_BLOCK = 32
CMP_STRIDE = 16
CMP_HIDDEN = 128
SEL_BLOCK = 64
TOP_N = 16
N_INIT_BLOCKS = 1
N_LOCAL_BLOCKS = 2
WINDOW = 512
QBLK = 128
GMLP_GROUPS = 4
CHUNK = 128
GMLP_GROUP_WIDTH = 128
GMLP_WIDTH = GMLP_GROUPS * GMLP_GROUP_WIDTH
N_BRANCH = 2
IN_WIDTH = ATTN_WIDTH + 6 * KV_WIDTH + 3 * N_HEADS + ATTN_WIDTH + 3 * GMLP_WIDTH + N_BRANCH * D_MODEL
NEG = -1e30
BIG = 1e30
EPS = 1e-6

kernel_name = 'nsa_gmlp_gated_hybrid_step'

def rmsnorm(x, g):
    xf = x.astype(jnp.float32)
    r = lax.rsqrt(jnp.mean(xf * xf, axis=-1, keepdims=True) + EPS)
    return (xf * r).astype(x.dtype) * g

def layernorm(x, g, b):
    xf = x.astype(jnp.float32)
    mu = jnp.mean(xf, axis=-1, keepdims=True)
    var = jnp.mean(jnp.square(xf - mu), axis=-1, keepdims=True)
    return ((xf - mu) * lax.rsqrt(var + EPS)).astype(x.dtype) * g + b

def rope(x, pos):
    inv = jnp.power(jnp.float32(ROPE_THETA), -jnp.arange(0, ROT_DIM, 2, dtype=jnp.float32) / ROT_DIM)
    ang = pos.astype(jnp.float32)[:, None] * inv[None, :]
    cos = jnp.cos(ang)[None, :, None, :].astype(x.dtype)
    sin = jnp.sin(ang)[None, :, None, :].astype(x.dtype)
    x1, x2, xr = x[..., :ROT_HALF], x[..., ROT_HALF:ROT_DIM], x[..., ROT_DIM:]
    return jnp.concatenate([x1 * cos - x2 * sin, x2 * cos + x1 * sin, xr], axis=-1)

def masked_softmax(s, mask):
    s = jnp.where(mask, s.astype(jnp.float32), NEG)
    return jnp.where(mask, jax.nn.softmax(s, axis=-1), 0.0)

def compress(rows, params):
    w1, b1, w2, b2 = params
    B, T, G, dh = rows.shape
    n_cmp = (T - CMP_BLOCK) // CMP_STRIDE + 1
    idx = jnp.arange(n_cmp)[:, None] * CMP_STRIDE + jnp.arange(CMP_BLOCK)[None, :]
    blocks = rows[:, idx].transpose(0, 1, 3, 2, 4).reshape(B, n_cmp, G, CMP_BLOCK * dh)
    return jax.nn.gelu(blocks @ w1 + b1) @ w2 + b2

def cmp_end_positions(n_cmp):
    return jnp.arange(n_cmp) * CMP_STRIDE + CMP_BLOCK - 1

def cmp_sel_overlap(n_cmp, n_sel):
    cs = jnp.arange(n_cmp)[:, None] * CMP_STRIDE
    ss = jnp.arange(n_sel)[None, :] * SEL_BLOCK
    ov = jnp.minimum(cs + CMP_BLOCK, ss + SEL_BLOCK) - jnp.maximum(cs, ss)
    return jnp.clip(ov, 0, None).astype(jnp.float32) / CMP_BLOCK

def nsa_core(q, qpos, kc, vc, cend, overlap, gather_sel, kw, vw, kpos):
    B, Tq, H, dh = q.shape
    q5 = q.reshape(B, Tq, KV_HEADS, HPG, dh) * (dh ** -0.5)
    s = jnp.einsum('bqgjd,bcgd->bgjqc', q5, kc)
    p = masked_softmax(s, (cend[None, :] <= qpos[:, None])[None, None, None])
    o_cmp = jnp.einsum('bgjqc,bcgd->bqgjd', p.astype(vc.dtype), vc).reshape(B, Tq, H, dh)
    imp = jnp.einsum('bgjqc,cs->bgqs', p, overlap)
    n_sel = overlap.shape[1]
    blk = jnp.arange(n_sel)[None, :]
    cur = (qpos // SEL_BLOCK)[:, None]
    valid = blk <= cur
    forced = ((blk <= cur) & (blk > cur - N_LOCAL_BLOCKS)) | (blk < N_INIT_BLOCKS)
    score = jnp.where(forced, BIG, jnp.where(valid, imp, NEG))
    _, idx = lax.top_k(score, min(TOP_N, n_sel))
    kg, vg = gather_sel(idx)
    n_top = idx.shape[-1]
    key_pos = idx[..., None] * SEL_BLOCK + jnp.arange(SEL_BLOCK)
    msel = (key_pos <= qpos[None, None, :, None, None]).reshape(B, KV_HEADS, 1, Tq, n_top * SEL_BLOCK)
    s = jnp.einsum('bqgjd,bgqnkd->bgjqnk', q5, kg).reshape(B, KV_HEADS, HPG, Tq, n_top * SEL_BLOCK)
    p = masked_softmax(s, msel)
    o_sel = jnp.einsum('bgjqm,bgqmd->bqgjd', p.astype(vg.dtype), vg.reshape(B, KV_HEADS, Tq, n_top * SEL_BLOCK, dh)).reshape(B, Tq, H, dh)
    s = jnp.einsum('bqgjd,bkgd->bgjqk', q5, kw)
    mw = (kpos[None, :] <= qpos[:, None]) & (kpos[None, :] > qpos[:, None] - WINDOW) & (kpos[None, :] >= 0)
    p = masked_softmax(s, mw[None, None, None])
    o_win = jnp.einsum('bgjqk,bkgd->bqgjd', p.astype(vw.dtype), vw).reshape(B, Tq, H, dh)
    return o_cmp, o_sel, o_win

def in_project(x, pos, lw):
    B, T, _ = x.shape
    h = rmsnorm(x, lw['norm_g'])
    proj = h @ lw['w_in']
    sizes = [ATTN_WIDTH] + [KV_WIDTH] * 6 + [3 * N_HEADS, ATTN_WIDTH, GMLP_WIDTH, GMLP_WIDTH, GMLP_WIDTH, N_BRANCH * D_MODEL]
    offs = np.cumsum(sizes)[:-1].tolist()
    q, k_cmp, v_cmp, k_sel, v_sel, k_win, v_win, gl, za, u, v, zb, r = jnp.split(proj, offs, axis=-1)
    kvh = lambda t: t.reshape(B, T, KV_HEADS, HEAD_DIM)
    q = rope(q.reshape(B, T, N_HEADS, HEAD_DIM), pos)
    return (q, kvh(k_cmp), kvh(v_cmp), rope(kvh(k_sel), pos), kvh(v_sel), rope(kvh(k_win), pos), kvh(v_win), gl, za, u, v, zb, r)

def spatial_gate(v, w_s, b_s):
    B, T, _ = v.shape
    n_chunk = -(-T // CHUNK)
    v = jnp.pad(v, ((0, 0), (0, n_chunk * CHUNK - T), (0, 0))).reshape(B, n_chunk, CHUNK, GMLP_GROUPS, GMLP_GROUP_WIDTH)
    tri = jnp.tril(jnp.ones((CHUNK, CHUNK), dtype=bool))
    w = jnp.where(tri[None], w_s, 0.0).astype(v.dtype)
    out = jnp.einsum('gts,bcsgd->bctgd', w, v) + b_s.T[None, None, :, :, None].astype(v.dtype)
    return out.reshape(B, n_chunk * CHUNK, GMLP_WIDTH)[:, :T]

def mixer_out(x, o_cmp, o_sel, o_win, gl, za, u, v, zb, r, lw):
    B, T, _ = x.shape
    g = jax.nn.sigmoid(gl.astype(jnp.float32)).astype(x.dtype).reshape(B, T, N_HEADS, 3)
    o = g[..., 0:1] * o_cmp + g[..., 1:2] * o_sel + g[..., 2:3] * o_win
    pa = (o.reshape(B, T, ATTN_WIDTH) * jax.nn.silu(za)) @ lw['w_pa']
    v_n = layernorm(jax.nn.gelu(v), lw['v_norm_g'], lw['v_norm_b'])
    sgu = jax.nn.gelu(u) * spatial_gate(v_n, lw['w_spatial'], lw['b_spatial'])
    pb = (sgu * jax.nn.silu(zb)) @ lw['w_pb']
    ra, rb = jnp.split(r, 2, axis=-1)
    merged = jax.nn.sigmoid(ra) * pa + jax.nn.sigmoid(rb) * pb
    return x + merged @ lw['w_o'], v_n

def prompt_layer(x, lw):
    B, S, _ = x.shape
    pos = jnp.arange(S)
    q, k_cmp, v_cmp, k_sel, v_sel, k_win, v_win, gl, za, u, v, zb, r = in_project(x, pos, lw)
    kc = compress(k_cmp, lw['cmp_k'])
    n_cmp = kc.shape[1]
    cend = cmp_end_positions(n_cmp)
    kc = rope(kc, cend)
    vc = compress(v_cmp, lw['cmp_v'])
    n_sel = S // SEL_BLOCK
    overlap = cmp_sel_overlap(n_cmp, n_sel)
    k_sel_t = k_sel.reshape(B, n_sel, SEL_BLOCK, KV_HEADS, HEAD_DIM).transpose(0, 3, 1, 2, 4)
    v_sel_t = v_sel.reshape(B, n_sel, SEL_BLOCK, KV_HEADS, HEAD_DIM).transpose(0, 3, 1, 2, 4)
    bidx = jnp.arange(B)[:, None, None, None]
    gidx = jnp.arange(KV_HEADS)[None, :, None, None]

    def gather_sel(idx):
        return k_sel_t[bidx, gidx, idx], v_sel_t[bidx, gidx, idx]

    pad = ((0, 0), (WINDOW, 0), (0, 0), (0, 0))
    kw_pad, vw_pad = jnp.pad(k_win, pad), jnp.pad(v_win, pad)
    n_qb = S // QBLK
    q_blocks = q.reshape(B, n_qb, QBLK, N_HEADS, HEAD_DIM).transpose(1, 0, 2, 3, 4)

    def block_fn(args):
        i, qb = args
        start = i * QBLK
        qpos = start + jnp.arange(QBLK)
        kw = lax.dynamic_slice_in_dim(kw_pad, start, WINDOW + QBLK, axis=1)
        vw = lax.dynamic_slice_in_dim(vw_pad, start, WINDOW + QBLK, axis=1)
        kpos = start - WINDOW + jnp.arange(WINDOW + QBLK)
        return nsa_core(qb, qpos, kc, vc, cend, overlap, gather_sel, kw, vw, kpos)

    o_blocks = lax.map(block_fn, (jnp.arange(n_qb), q_blocks))
    o_cmp, o_sel, o_win = [t.transpose(1, 0, 2, 3, 4).reshape(B, S, N_HEADS, HEAD_DIM) for t in o_blocks]
    x_new, _ = mixer_out(x, o_cmp, o_sel, o_win, gl, za, u, v, zb, r, lw)
    wc = min(WINDOW, S)
    return x_new, (k_cmp, v_cmp, k_sel, v_sel, k_win[:, S - wc:], v_win[:, S - wc:])

def sample_layer(x, ck_cmp, cv_cmp, ck_sel, cv_sel, ck_win, cv_win, page_table, lw):
    Bd, Tn, _ = x.shape
    n_pages = page_table.shape[1]
    past = n_pages * PAGE_SIZE
    pos = past + jnp.arange(Tn)
    q, k_cmp, v_cmp, k_sel, v_sel, k_win, v_win, gl, za, u, v, zb, r = in_project(x, pos, lw)

    def gather_pages(pool):
        return pool[page_table].reshape(Bd, past, KV_HEADS, HEAD_DIM)

    kc = compress(jnp.concatenate([gather_pages(ck_cmp), k_cmp], axis=1), lw['cmp_k'])
    n_cmp = kc.shape[1]
    cend = cmp_end_positions(n_cmp)
    kc = rope(kc, cend)
    vc = compress(jnp.concatenate([gather_pages(cv_cmp), v_cmp], axis=1), lw['cmp_v'])
    n_past_blk = past // SEL_BLOCK
    n_tail = -(-Tn // SEL_BLOCK)
    overlap = cmp_sel_overlap(n_cmp, n_past_blk + n_tail)
    bpp = PAGE_SIZE // SEL_BLOCK
    pk = ck_sel.reshape(-1, bpp, SEL_BLOCK, KV_HEADS, HEAD_DIM)
    pv = cv_sel.reshape(-1, bpp, SEL_BLOCK, KV_HEADS, HEAD_DIM)
    tpad = ((0, 0), (0, n_tail * SEL_BLOCK - Tn), (0, 0), (0, 0))
    tk = jnp.pad(k_sel, tpad).reshape(Bd, n_tail, SEL_BLOCK, KV_HEADS, HEAD_DIM).transpose(0, 3, 1, 2, 4)
    tv = jnp.pad(v_sel, tpad).reshape(Bd, n_tail, SEL_BLOCK, KV_HEADS, HEAD_DIM).transpose(0, 3, 1, 2, 4)
    bidx = jnp.arange(Bd)[:, None, None, None]
    gidx = jnp.arange(KV_HEADS)[None, :, None, None]

    def gather_sel(idx):
        phys = page_table[bidx, jnp.minimum(idx // bpp, n_pages - 1)]
        sub = idx % bpp
        ti = jnp.clip(idx - n_past_blk, 0, n_tail - 1)
        is_tail = (idx >= n_past_blk)[..., None, None]
        kg = jnp.where(is_tail, tk[bidx, gidx, ti], pk[phys, sub, :, gidx])
        vg = jnp.where(is_tail, tv[bidx, gidx, ti], pv[phys, sub, :, gidx])
        return kg, vg

    wc = ck_win.shape[1]
    kw = jnp.concatenate([ck_win, k_win], axis=1)
    vw = jnp.concatenate([cv_win, v_win], axis=1)
    kpos = past - wc + jnp.arange(wc + Tn)
    o_cmp, o_sel, o_win = nsa_core(q, pos, kc, vc, cend, overlap, gather_sel, kw, vw, kpos)
    x_new, v_n = mixer_out(x, o_cmp, o_sel, o_win, gl, za, u, v, zb, r, lw)
    return x_new, (k_cmp, v_cmp, k_sel, v_sel, kw[:, kw.shape[1] - wc:], vw[:, vw.shape[1] - wc:], v_n)

def setup_inputs(seed: int = 0) -> dict:
    key = jax.random.key(seed)
    ks = jax.random.split(key, 32)
    f32 = jnp.float32
    nrm = lambda k, shape, scale: scale * jax.random.normal(k, shape, f32)
    n_pages = PAST_LEN // PAGE_SIZE
    n_used = DEC_BATCH * n_pages
    n_phys = n_used + max(1, n_used // 4)
    win_cache = min(WINDOW, PAST_LEN)
    pool_shape = (DEPTH, n_phys, PAGE_SIZE, KV_HEADS, HEAD_DIM)
    win_shape = (DEPTH, DEC_BATCH, win_cache, KV_HEADS, HEAD_DIM)
    perm = jax.random.permutation(ks[8], n_phys)
    page_table = perm[:n_used].reshape(DEC_BATCH, n_pages).astype(jnp.int32)
    L = DEPTH
    return {
        'x_prompt': nrm(ks[0], (BATCH, SEQ, D_MODEL), 1.0),
        'x_sample': nrm(ks[1], (DEC_BATCH, DEC_SEQ, D_MODEL), 1.0),
        'cache_k_cmp': nrm(ks[2], pool_shape, 1.0),
        'cache_v_cmp': nrm(ks[3], pool_shape, 1.0),
        'cache_k_sel': nrm(ks[4], pool_shape, 1.0),
        'cache_v_sel': nrm(ks[5], pool_shape, 1.0),
        'cache_k_win': nrm(ks[6], win_shape, 1.0),
        'cache_v_win': nrm(ks[7], win_shape, 1.0),
        'page_table': page_table,
        'norm_g': 1.0 + nrm(ks[9], (L, D_MODEL), 0.1),
        'w_in': nrm(ks[10], (L, D_MODEL, IN_WIDTH), D_MODEL ** -0.5),
        'cmp_k_w1': nrm(ks[11], (L, CMP_BLOCK * HEAD_DIM, CMP_HIDDEN), (CMP_BLOCK * HEAD_DIM) ** -0.5),
        'cmp_k_b1': nrm(ks[12], (L, CMP_HIDDEN), 0.02),
        'cmp_k_w2': nrm(ks[13], (L, CMP_HIDDEN, HEAD_DIM), CMP_HIDDEN ** -0.5),
        'cmp_k_b2': nrm(ks[14], (L, HEAD_DIM), 0.02),
        'cmp_v_w1': nrm(ks[15], (L, CMP_BLOCK * HEAD_DIM, CMP_HIDDEN), (CMP_BLOCK * HEAD_DIM) ** -0.5),
        'cmp_v_b1': nrm(ks[16], (L, CMP_HIDDEN), 0.02),
        'cmp_v_w2': nrm(ks[17], (L, CMP_HIDDEN, HEAD_DIM), CMP_HIDDEN ** -0.5),
        'cmp_v_b2': nrm(ks[18], (L, HEAD_DIM), 0.02),
        'v_norm_g': 1.0 + nrm(ks[19], (L, GMLP_WIDTH), 0.1),
        'v_norm_b': nrm(ks[20], (L, GMLP_WIDTH), 0.02),
        'w_spatial': nrm(ks[21], (L, GMLP_GROUPS, CHUNK, CHUNK), CHUNK ** -0.5),
        'b_spatial': 1.0 + nrm(ks[22], (L, GMLP_GROUPS, CHUNK), 0.1),
        'w_pa': nrm(ks[23], (L, ATTN_WIDTH, D_MODEL), ATTN_WIDTH ** -0.5),
        'w_pb': nrm(ks[24], (L, GMLP_WIDTH, D_MODEL), GMLP_WIDTH ** -0.5),
        'w_o': nrm(ks[25], (L, D_MODEL, D_MODEL), D_MODEL ** -0.5),
        'final_g': 1.0 + nrm(ks[26], (D_MODEL,), 0.1),
    }

def reference(x_prompt, x_sample, cache_k_cmp, cache_v_cmp, cache_k_sel, cache_v_sel, cache_k_win, cache_v_win, page_table,
              norm_g, w_in, cmp_k_w1, cmp_k_b1, cmp_k_w2, cmp_k_b2, cmp_v_w1, cmp_v_b1, cmp_v_w2, cmp_v_b2,
              v_norm_g, v_norm_b, w_spatial, b_spatial, w_pa, w_pb, w_o, final_g):
    hp, hs = x_prompt, x_sample
    st_p = [[] for _ in range(6)]
    st_s = [[] for _ in range(7)]
    for l in range(DEPTH):
        lw = {
            'norm_g': norm_g[l], 'w_in': w_in[l],
            'cmp_k': (cmp_k_w1[l], cmp_k_b1[l], cmp_k_w2[l], cmp_k_b2[l]),
            'cmp_v': (cmp_v_w1[l], cmp_v_b1[l], cmp_v_w2[l], cmp_v_b2[l]),
            'v_norm_g': v_norm_g[l], 'v_norm_b': v_norm_b[l],
            'w_spatial': w_spatial[l], 'b_spatial': b_spatial[l],
            'w_pa': w_pa[l], 'w_pb': w_pb[l], 'w_o': w_o[l],
        }
        hp, sp = prompt_layer(hp, lw)
        hs, ss = sample_layer(hs, cache_k_cmp[l], cache_v_cmp[l], cache_k_sel[l], cache_v_sel[l],
                              cache_k_win[l], cache_v_win[l], page_table, lw)
        for lst, t in zip(st_p, sp):
            lst.append(t)
        for lst, t in zip(st_s, ss):
            lst.append(t)
    y_prompt = rmsnorm(hp, final_g)
    y_sample = rmsnorm(hs, final_g)
    p_k_cmp, p_v_cmp, p_k_sel, p_v_sel, p_k_win, p_v_win = [jnp.stack(t) for t in st_p]
    s_k_cmp, s_v_cmp, s_k_sel, s_v_sel, s_k_win, s_v_win, s_v_chunk = [jnp.stack(t) for t in st_s]
    return (y_prompt, y_sample, p_k_cmp, p_v_cmp, p_k_sel, p_v_sel, p_k_win, p_v_win,
            s_k_cmp, s_v_cmp, s_k_sel, s_v_sel, s_k_win, s_v_win, s_v_chunk)


_drawn_inputs = setup_inputs


def setup_inputs(seed=0):
    import zlib

    import numpy as np

    out = dict(_drawn_inputs(seed))
    spreads = {}
    factors = {'cache_k_cmp': 6.988,
     'cache_v_cmp': 3.702,
     'cache_k_sel': 8.0,
     'cache_v_sel': 6.482,
     'cmp_k_w1': 3.806,
     'cmp_k_b1': 54.286,
     'cmp_k_w2': 3.596,
     'cmp_k_b2': 200.0,
     'cmp_v_b1': 28.763,
     'cmp_v_b2': 8.0,
     'v_norm_b': 2.942,
     'b_spatial': 2.78}
    for name, (base, spread) in spreads.items():
        noise = np.random.default_rng([zlib.crc32(name.encode()), seed]).standard_normal(out[name].shape)
        drawn = base * np.exp(spread * noise) if base else spread * noise
        out[name] = __import__('jax').numpy.asarray(drawn.astype(out[name].dtype))
    for name, factor in factors.items():
        out[name] = (out[name] * factor).astype(out[name].dtype)
    return out
```

```python
from contextlib import ExitStack

import numpy as np
import concourse.bass as bass
from concourse import mybir

F32 = mybir.dt.float32
F32R = mybir.dt.float32r
I32 = mybir.dt.int32
U32 = mybir.dt.uint32
ALU = mybir.AluOpType
ACT = mybir.ActivationFunctionType
AX = mybir.AxisListType.X

P = 128
D = 1024
KD = D // P
TP, NB, TQ = 512, 8, 4
TS = NB * TQ
T = TP + TS
NT = TP // P
HALF = T // 2
G, J, H, DH = 2, 4, 8, 64
PAST, PAGE = 1024, 128
NCS = (PAST + TQ - 32) // 16 + 1
NCP = (TP - 32) // 16 + 1
NSEL = PAST // 64 + 1
QB = 4
NQ = NB // QB
NEG = -1e30
EPS = 1e-6
SCALE = DH ** -0.5
ROT = 16
THETA = 500000.0

C_Q, C_KCMP, C_KSEL, C_KWIN, C_GL, C_ZA, C_U, C_V, C_ZB, C_R = 0, 512, 768, 1024, 1280, 1304, 1816, 2328, 2840, 3352
SW = 280
SLOTS = [("B0", "tm", C_KCMP, 256), ("B1", "tm", C_KSEL, 256), ("C0", "tm", C_KWIN, 280),
         ("A0", "tm", C_Q, 256), ("A1", "tm", C_Q + 256, 256), ("V0", "tm", C_V, 256), ("V1", "tm", C_V + 256, 256),
         ("U0", "tr", C_U, 256), ("U1", "tr", C_U + 256, 256),
         ("ZA0", "tr", C_ZA, 256), ("ZA1", "tr", C_ZA, 256),
         ("ZB0", "tr", C_ZB, 256), ("ZB1", "tr", C_ZB + 256, 256)] + \
        [(f"RA{n}", "tr", C_R + 256 * n, 256) for n in range(4)] + \
        [(f"RB{n}", "tr", C_R + D + 256 * n, 256) for n in range(4)] + \
        [(f"WO{n}", "wo", 256 * n, 256) for n in range(4)]
SLOT = {s[0]: n for n, s in enumerate(SLOTS)}
NRAW = 3

CONSTS = {}


def _layout(items):
    at = 0
    for name, width in items:
        CONSTS[name] = (at, at + width)
        at += width
    return at


NC_CONST = _layout([("ident", 128), ("causal", 512), ("cos_tok", 5 * ROT), ("sin_tok", 5 * ROT), ("cos_blk", NCS),
                    ("sin_blk", NCS), ("cmp_mask", NT * NCP), ("row_mask", 1), ("pick_rows", NQ * P),
                    ("pick_head", H), ("new_mask", NQ * TS), ("win_mask", TQ), ("overlap", NSEL), ("block_no", 14),
                    ("repeat4", TS), ("same_batch", TS), ("group_mod", 1)])


def constants():
    c = np.zeros((P, NC_CONST), np.float32)

    def put(name, a):
        a = np.asarray(a, np.float32)
        c[:a.shape[0], CONSTS[name][0]:CONSTS[name][0] + a.shape[1]] = a

    p = np.arange(P)
    put("ident", np.eye(P))
    causal = np.zeros((P, 512), np.float32)
    causal[:, 384:] = np.where(np.arange(P)[None] <= p[:, None], 0.0, NEG)
    put("causal", causal)
    inv = np.power(np.float32(THETA), -np.arange(0, ROT, 2, dtype=np.float32) / np.float32(ROT)).astype(np.float32)
    cos, sin = np.zeros((P, 5, ROT), np.float32), np.zeros((P, 5, ROT), np.float32)
    for i in range(5):
        pos = (i * P + p if i < NT else PAST + p % TQ).astype(np.float32)
        ang = pos[:, None] * inv[None]
        cos[:, i], sin[:, i] = np.tile(np.cos(ang), (1, 2)), np.tile(np.sin(ang), (1, 2))
    put("cos_tok", cos.reshape(P, -1))
    put("sin_tok", sin.reshape(P, -1))
    ang = (np.arange(NCS) * 16 + 31).astype(np.float32)[None] * inv[:, None]
    cb, sb = np.ones((DH, NCS), np.float32), np.zeros((DH, NCS), np.float32)
    cb[:8], cb[8:16], sb[:8], sb[8:16] = np.cos(ang), np.cos(ang), -np.sin(ang), np.sin(ang)
    put("cos_blk", np.tile(cb, (2, 1)))
    put("sin_blk", np.tile(sb, (2, 1)))
    blk = np.arange(NCP) * 16 + 31
    put("cmp_mask", np.concatenate([np.where(blk[None] <= (i * P + p)[:, None], 0.0, NEG) for i in range(NT)], 1))
    put("row_mask", (p >= 31)[:, None])
    row_b, row_h, row_t = p // 32, p % 32 // 4, p % 4
    tok = np.arange(TS)
    for q in range(NQ):
        b = q * QB + row_b
        a, o = CONSTS["pick_rows"][0] + q * P, CONSTS["new_mask"][0] + q * TS
        c[:TS, a:a + P] = tok[:, None] == (b * TQ + row_t)[None]
        ok = (tok[None] // TQ == b[:, None]) & (tok[None] % TQ <= row_t[:, None])
        c[:, o:o + TS] = np.where(ok, 0.0, NEG)
    put("pick_head", row_h[:, None] == np.arange(H)[None])
    put("win_mask", np.where(np.arange(TQ)[None] <= row_t[:, None], NEG, 0.0))
    cs, ss = np.arange(NCS)[:, None] * 16, np.arange(NSEL)[None] * 64
    put("overlap", np.clip(np.minimum(cs + 32, ss + 64) - np.maximum(cs, ss), 0, None) / 32.0)
    put("block_no", np.tile(np.arange(1, 15), (P, 1)))
    put("repeat4", np.arange(TQ)[:, None] == tok[None] % TQ)
    put("same_batch", tok[:, None] // TQ == tok[None] // TQ)
    put("group_mod", (p % 16)[:, None])
    return c


PARAMS = {}


def _params(items):
    at = 0
    for name, width in items:
        PARAMS[name] = (at, at + width)
        at += width
    return at


N_PARAM = _params([("norm_g", D), ("v_g", 512), ("v_b", 512), ("b_sp", 512), ("w2k", DH), ("w2kr", DH), ("w2v", DH),
                   ("b1k", 1), ("b1v", 1), ("b2k", 1), ("b2kr", 1), ("b2v", P)])


def plan():
    order, groups = [], []
    for s, (name, kind, _, _) in enumerate(SLOTS):
        if kind == "wo":
            continue
        groups += [("main", s, a, b) for a, b in ([(i, 0) for i in range(NT + 1)] if kind == "tm"
                                                  else [(a, b) for a in range(2) for b in range(2)])]
    state = {"n": 0}

    def main(count):
        for _ in range(count):
            if state["n"] >= len(groups):
                return
            g = groups[state["n"]]
            order.append(g)
            state["n"] += 1
            first = next(n for n, x in enumerate(groups) if x[1] == g[1])
            at = state["n"] - 1 - first
            if g[1] >= 1 and at < 2:
                order.append(("split", g[1] + 1, at))

    order += [("norm",), ("split", 0, 0), ("split", 0, 1)]
    order += [("hT", i) for i in range(NT + 1)]
    order += [("split", 1, 0), ("split", 1, 1)]
    main(5)
    order += [("out_cmp",), ("wsT",)]
    main(5)
    order += [("rope", 0)]
    main(3)
    order += [("kT", 0)]
    main(2)
    order += [("rope", 1), ("gates",)]
    main(3)
    order += [("kT", 1), ("kTs",), ("wbd",)]
    main(3)
    order += [("gr",)]
    main(4)
    order += [("rope", 2)]
    main(4)
    order += [("qT", i) for i in range(NT)] + [("qTs",)]
    main(6)
    for c in range(6):
        if c == 0:
            order += [("xt", c, n) for n in range(8)] + [("ln",), ("hid", c)]
            order += [("sp", i) for i in range(NT + 1)]
        else:
            order += [("xt", c, n) for n in range(8 if c % 3 < 2 else 1)] + [("kc", c - 1)]
            main(1)
            order += [("hid", c)]
    main(1)
    order += [("kc", 5)]
    for q in range(NQ):
        for b in range(QB * q, QB * q + QB):
            order += [("qkT", b)]
            main(1)
            order += [("qkS", b)]
        order += [("s_max", q)]
        main(1)
        order += [("s_turn", q)]
        main(1 if q == 0 else 0)
        order += [("s_imp", q)]
        main(2 - q)
        order += [("s_exp", q)]
        main(2 - q)
        order += [("s_scale", q)]
        main(1 - q)
        order += [("s_pv", q), ("s_out", q)]
    assert state["n"] == 59
    units = [(i, g, y) for i in range(NT) for g in range(G) for y in range(2)]
    limit = 35 + 8 + 16 + 16 + 10
    for u, (i, g, y) in enumerate(units):
        if g == 0 and y == 0:
            order += [("cs", i)]
        order += [("ps", u)]
        main(min(1, limit - state["n"]))
        if u:
            order += [("pt", u - 1, kt) for kt in range(units[u - 1][0] + 2)]
        if g == 0 and y == 0:
            order += [("oz", i - 1)] if i else []
            order += [("cn", i)]
        order += [("pn", u)]
        main(min(1, limit - state["n"]))
        if g == 0 and y == 0:
            order += [("ct", i, 0), ("ct", i, 1)]
    order += [("pt", len(units) - 1, kt) for kt in range(NT + 1)]
    order += [("oz", NT - 1)]
    main(len(groups))
    order += [("load_wp", 0), ("load_wp", 1)]
    pending = None
    for n in range(4):
        for d in range(4):
            for hf in range(2):
                order.append(("main", "wp", n, d, hf))
                if pending:
                    order.append(pending)
                    pending = None
                if n % 2:
                    pending = ("mlo", n // 2 * 4 + d, hf)
                if n == 0 and d == 0:
                    order.append(("split", SLOT["WO1"], hf))
        if n < 2:
            order.append(("load_wp", n + 2))
    order.append(pending)
    order.append(("load_x",))
    for c in range(4):
        for i in [4, 0, 1, 2, 3]:
            order.append(("main", SLOT["WO0"] + c, i, 0))
            at = [4, 0, 1, 2, 3].index(i)
            if 1 <= c < 3 and at < 2:
                order.append(("split", SLOT["WO0"] + c + 1, at))
            if c == 3:
                order.append(("fin", i))
    return order, units


ORDER, UNITS = plan()
MAIN = [s for s in ORDER if s[0] == "main"]
MAIN_AT = {s: n for n, s in enumerate(MAIN)}


def freed_by(s):
    if s[1] == "wp" or SLOTS[s[1]][1] == "wo" or SLOTS[s[1]][0][0] == "Z":
        return "dve"
    return "act"


def t_uses(s):
    kind = s[0]
    if kind == "hT":
        return ["dve", "dve"]
    if kind in ("wsT", "wbd", "kT", "kTs", "qTs", "gr", "sp", "s_turn", "s_imp", "s_out", "cs"):
        return ["dve"]
    if kind == "qT":
        return ["act"]
    if kind == "xt":
        return ["act" if s[2] % 2 else "dve"]
    if kind == "qkT":
        return ["act", "dve", "act"]
    if kind == "s_pv":
        return ["dve", "act", "dve", "act"]
    if kind == "ct":
        return ["act" if s[2] else "dve"]
    if kind == "pt" and s[2] <= UNITS[s[1]][0]:
        return ["act" if (s[1] + s[2]) % 2 else "dve"]
    return []


T_USE, T_AT = [], {}
for _s in ORDER:
    T_AT[_s] = len(T_USE)
    T_USE += t_uses(_s)

RING = 3
LOADS = [(w, b) for w in ("kc", "vc") for b in list(range(NB)) + ["p"]] + \
        [(w, b) for b in range(NB) for w in ("ks", "kw")]
LOAD_AT = {x: n for n, x in enumerate(LOADS)}
PT_AT = {}
for _s in ORDER:
    if _s[0] == "ct" or (_s[0] == "pt" and _s[2] <= UNITS[_s[1]][0]):
        PT_AT[_s] = len(PT_AT)
NPT = 4


def part(c):
    return ("kc" if c < 3 else "vc"), c % 3


def packed_used(n):
    w, b = LOADS[n]
    c = (0 if w == "kc" else 3) + (2 if b == "p" else b // QB)
    return T_AT[("xt", c, 0 if b == "p" else 2 * (b % QB) + 1)] + 1


def load_freed(n):
    w, b = LOADS[n - RING]
    return T_AT[("qkT", b)] + (2 if w == "ks" else 3)


def raw_count(r):
    return sum(32 if SLOTS[n // 2][0].startswith("ZA") else 16 for n in range(r % NRAW, r + 1, NRAW))


def slot_used(sl):
    return max(n for n, x in enumerate(MAIN) if x[1] == sl) + 1


def hid_count(c):
    return [0, 2, 4, 5, 7, 9, 10][c]


FN_AT = {x: n for n, x in enumerate(x for x in MAIN if x[1] != "wp" and SLOTS[x[1]][0][0] in "UZ")}
ROPE_STEPS = [12, 24, 48]
N_OUT = 11


def nsa_gmlp_layer(nc, x_p, x_s, ck_cmp, cv_cmp, ck_sel, cv_sel, ck_win, cv_win, pages, w_in, w1k, w1v, w_sp,
                   w_pa, w_pb, w_o, final_g, params, consts, outs):
    (y_p, y_s, pk_cmp, pv_cmp, pk_sel, pv_sel, pk_win, pv_win,
     sk_cmp, sv_cmp, sk_sel, sv_sel, sk_win, sv_win, s_chunk) = outs
    ctx = ExitStack()
    with ctx:
        def sb(name, shape, dt=F32):
            return ctx.enter_context(nc.sbuf_tensor(name, shape, dt))

        def sem(name):
            return ctx.enter_context(nc.semaphore(name))

        h_hi, h_lo = sb("h_hi", [P, KD, T], F32R), sb("h_lo", [P, KD, T], F32R)
        w_hi, w_lo = sb("w_hi", [P, 2, KD, SW], F32R), sb("w_lo", [P, 2, KD, SW], F32R)
        raw = sb("raw", [P, NRAW, KD // 2, SW])
        v_tok = sb("v_tok", [P, 2, NT + 1, P])
        qT = sb("qT", [P, J, TP])
        k_pad = sb("k_pad", [P, 2, G, TP])
        sg = sb("sg", [P, 4, T])
        za = sb("za", [P, 4, T])
        cst = sb("cst", [P, NC_CONST])
        prm = sb("prm", [P, N_PARAM])
        wsT = sb("wsT", [P, 4, P])
        w_bd = sb("w_bd", [TS, 4, TS])
        kcT = sb("kcT", [P, NB, NCS])
        vc = sb("vc", [NCS, NB, P])
        kcp = sb("kcp", [P, G, NCP])
        vcp = sb("vcp", [NCP, P])
        gate = sb("gate", [P, NT + 1, 3 * H])
        gate_row = sb("gate_row", [P, NQ, 3])
        q_bd = sb("q_bd", [P, NB, G * J * TQ])
        k_newT = sb("k_newT", [P, 2, TS])
        o_row = sb("o_row", [P, P])
        tmp = sb("tmp", [P, 2, HALF])
        st = sb("st", [P, 128])
        pj_sum = sb("pj_sum", [NCS, 160])
        pick = sb("pick", [P, 14])
        penalty_sb = sb("penalty", [P, P])
        pages_sb = sb("pages_sb", [P, NB], I32)
        rows_sb = sb("rows_sb", [P, NB], U32)
        U = sb("U", [P, 13824])

        def cs(name, rows=P):
            return cst[0:rows, CONSTS[name][0]:CONSTS[name][1]]

        def pm(name, rows=P):
            return prm[0:rows, PARAMS[name][0]:PARAMS[name][1]]

        ident = cs("ident")
        penalty = penalty_sb[:, :]
        x_in = U[:, 0:5120].rearrange("p (i c) -> p i c", i=5)
        junk = U[:, 5120:6144]
        kq = U[:, 0:5120].rearrange("p (i c) -> p i c", i=5)
        vg = U[:, 5120:7680].rearrange("p (i c) -> p i c", i=5)
        ws_raw = U[:, 7680:8192].rearrange("p (g s) -> p g s", g=4)
        ring = U[:, 8192:11264].rearrange("p (r c) -> p r c", r=RING)
        w1_at = [U[:, 11264:13312].rearrange("p (j n) -> p j n", j=16), U[:, 4096:6144].rearrange("p (j n) -> p j n", j=16)]
        packed = za[:, :, :].rearrange("p j t -> p (j t)")[:, 0:2048].rearrange("p (r c) -> p r c", r=2)
        xt = U[:, 0:4096].rearrange("p (q g m) -> p q g m", q=4, g=G)
        xtp = U[:, 0:512].rearrange("p (q g m) -> p q g m", q=4, g=G)
        hid = U[:, 13312:13312 + 504].rearrange("p (g n) -> p g n", g=G)
        t1, t2 = U[:, 7680:7680 + 252], U[:, 7936:7936 + 252]
        rt = U[:, 13312:13824]
        vs = U[:, 0:4096].rearrange("p (b s d) -> p b s d", b=QB, s=8)
        vw = U[:, 4096:6144].rearrange("p (b s d) -> p b s d", b=QB, s=4)
        kt_s = U[:, 6144:7168]
        kt_w = U[:, 7168:7680]
        ptr = [U[:, 7680:8192], U[:, 12928:13440]]
        pts = U[:, 13440:13824]
        ps = U[:, 11264:12928]
        SEL, WIN, CMP = 0, 1056, 1600
        pb = U[:, 0:4096].rearrange("p (b j k) -> p b j k", b=2, j=J)
        ptb = U[:, 4096:6144].rearrange("p (r n) -> p r n", r=NPT)
        cp = U[:, 6144:6144 + J * G * NCP]
        sig = U[:, 5120:13824].rearrange("p (n t) -> p n t", t=T)

        def sig_at(b, d):
            n = 3 + 8 * b + d
            return sig[:, n if n < 16 else n - 16, :]

        wp = U[:, 0:4096].rearrange("p (r k c) -> p r k c", r=2, k=4)
        xr = U[:, 0:5120].rearrange("p (i c) -> p i c", i=5)

        bank = [ctx.enter_context(nc.psum_tensor(n, [P, 512], F32)) for n in ("m0", "m1", "t0", "t1", "s0", "s1", "s2", "o")]
        M, TB, S, O = bank[0:2], bank[2:4], bank[4:7], bank[7]

        x_loaded, const_loaded, small_loaded = sem("x_loaded"), sem("const_loaded"), sem("small_loaded")
        raw_loaded = [sem(f"raw_loaded{n}") for n in range(NRAW)]
        w1_loaded = [sem("w1k_loaded"), sem("w1v_loaded")]
        ring_loaded = [sem(f"ring_loaded{n}") for n in range(RING)]
        v_loaded, wp_loaded = sem("v_loaded"), [sem("wp_loaded0"), sem("wp_loaded1")]
        xr_loaded, out_done, cmp_out = sem("xr_loaded"), sem("out_done"), sem("cmp_out")
        win_out, y_out = sem("win_out"), sem("y_out")
        rows_ready, ws_masked, rope_step = sem("rows_ready"), sem("ws_masked"), sem("rope_step")
        pads_zero, st_ready, mix_fn, pv_part, pt_used = (sem("pads_zero"), sem("st_ready"), sem("mix_fn"), sem("pv_part"),
                                                         sem("pt_used"))
        ssq_ready, root_in, root_done, h_ready = sem("ssq_ready"), sem("root_in"), sem("root_done"), sem("h_ready")
        hi_done, lo_done = sem("hi_done"), sem("lo_done")
        hT_hi, hT_lo = sem("hT_hi"), sem("hT_lo")
        main_done, main_act, main_dve = sem("main_done"), sem("main_act"), sem("main_dve")
        t_done, t_act, t_dve = sem("t_done"), sem("t_act"), sem("t_dve")
        gl_tanh, gate_ready = sem("gl_tanh"), sem("gate_ready")
        var_ready, std_ready, vn_ready = sem("var_ready"), sem("std_ready"), sem("vn_ready")
        wsT_ready, kT_ready, new_ready, qbd_ready = sem("wsT_ready"), sem("kT_ready"), sem("new_ready"), sem("qbd_ready")
        wbd_ready = sem("wbd_ready")
        repacked = sem("repacked")
        hid_sum, hid_ready, kc_done, kc_ready = sem("hid_sum"), sem("hid_ready"), sem("kc_done"), sem("kc_ready")
        act_fn = sem("act_fn")
        qk_done = sem("qk_done")
        s_bias, s_cexp, s_cp, s_pj, s_bias2, s_exp, s_p = (sem("s_bias"), sem("s_cexp"), sem("s_cp"), sem("s_pj"),
                                                           sem("s_bias2"), sem("s_exp"), sem("s_p"))
        o_done, o_row_ready, o_free = sem("o_done"), sem("o_row_ready"), sem("o_free")
        c_in, c_exp, c_p = sem("c_in"), sem("c_exp"), sem("c_p")
        p_scored, p_bias, p_masked, p_exp, p_scaled = (sem("p_scored"), sem("p_bias"), sem("p_masked"), sem("p_exp"),
                                                       sem("p_scaled"))
        mix_ready = sem("mix_ready")
        m_sum, m_hi, m_lo = sem("m_sum"), sem("m_hi"), sem("m_lo")
        f_ssq, f_ms, f_root, f_out = sem("f_ssq"), sem("f_ms"), sem("f_root"), sem("f_out")
        dve_step, act_step = sem("dve_step"), sem("act_step")

        def count(which, upto, engine):
            return sum(1 for e in which[:upto] if e == engine)

        main_by = [freed_by(s) for s in MAIN]

        def wait_main_bank(eng, n):
            if n >= 2:
                e = main_by[n - 2]
                eng.wait_ge(main_act if e == "act" else main_dve, count(main_by, n - 1, e))

        def wait_t_bank(eng, t):
            if t >= 2:
                e = T_USE[t - 2]
                eng.wait_ge(t_act if e == "act" else t_dve, count(T_USE, t - 1, e))

        def wait_evacuated(eng, t):
            e = T_USE[t]
            eng.wait_ge(t_act if e == "act" else t_dve, count(T_USE, t + 1, e))

        def wait_main_read(eng, s):
            n = MAIN_AT[s]
            e = main_by[n]
            eng.wait_ge(main_act if e == "act" else main_dve, count(main_by, n + 1, e))

        def wait_tmp_read(eng, k):
            s = list(FN_AT)[k]
            if SLOTS[s[1]][0].startswith("ZA"):
                wait_main_read(eng, s)
            else:
                eng.wait_ge(mix_fn, k + 1 - (8 if k >= 16 else 0))

        def tok(i):
            return slice(i * P, (i + 1) * P) if i < NT else slice(TP, T)

        def n_sp(i):
            return P if i < NT else TS

        def split_parts(sl, hf, r, w):
            ks = slice(4 * hf, 4 * hf + 4)
            hi, lo, x = w_hi[:, sl % 2, ks, 0:w], w_lo[:, sl % 2, ks, 0:w], raw[:, r, :, 0:w]
            if not SLOTS[sl][0].startswith("ZA"):
                return [(hi, lo, x)]
            xs = x.rearrange("p k (g j d) -> p k g j d", g=G, j=2)
            return [(*(a[:, :, j * P:(j + 1) * P].rearrange("p k (g d) -> p k g d", g=G) for a in (hi, lo)), xs[:, :, :, j, :])
                    for j in range(2)]

        def last_of(name):
            return ("main", SLOT[name], NT, 0)

        w_dram = w_in.rearrange("(k p) n -> p k n", p=P)
        wo_dram = w_o.rearrange("(k p) n -> p k n", p=P)

        block = ctx.enter_context(nc.Block())

        @block.sync
        def _(sp):
            def load_raw(r):
                s, hf = divmod(r, 2)
                if s >= len(SLOTS):
                    return
                name, kind, c0, w = SLOTS[s]
                if r >= NRAW:
                    sp.wait_ge(lo_done, r - NRAW + 1)
                dst = raw[:, r % NRAW, :, 0:w]
                ks = slice(4 * hf, 4 * hf + 4)
                if name.startswith("ZA"):
                    n = int(name[2])
                    for g in range(G):
                        a = c0 + g * 256 + n * 128
                        sp.dma_start(raw[:, r % NRAW, :, g * 128:g * 128 + 128],
                                     w_dram[:, ks, a:a + 128]).then_inc(raw_loaded[r % NRAW], 16)
                elif kind == "wo":
                    sp.dma_start(dst, wo_dram[:, ks, c0:c0 + w]).then_inc(raw_loaded[r % NRAW], 16)
                else:
                    sp.dma_start(dst, w_dram[:, ks, c0:c0 + w]).then_inc(raw_loaded[r % NRAW], 16)

            for i in range(NT):
                sp.dma_start(x_in[:, i, :], x_p[tok(i), :]).then_inc(x_loaded, 16)
            sp.dma_start(x_in[0:TS, NT, :], x_s).then_inc(x_loaded, 16)
            sp.dma_start(prm[:, 0:N_PARAM], params).then_inc(const_loaded, 16)
            sp.dma_start(cst[:, :], consts).then_inc(const_loaded, 16)
            for r in range(NRAW):
                load_raw(r)
            sp.dma_start(pages_sb[:, :], pages).then_inc(small_loaded, 16)
            sp.dma_start(ws_raw, w_sp).then_inc(small_loaded, 16)
            sp.dma_start(w1_at[0], w1k.rearrange("(j p) n -> p j n", p=P)).then_inc(w1_loaded[0], 16)
            n_win = 0
            for s in ORDER:
                if s[0] == "split":
                    load_raw(2 * s[1] + s[2] + NRAW)
                elif s == ("hid", 0):
                    sp.wait_ge(vn_ready, NT + 1)
                    sp.wait_ge(t_done, T_AT[("sp", NT)] + 1)
                    sp.wait_ge(out_done, 16 * N_OUT)
                    sp.dma_start(w1_at[1], w1v.rearrange("(j p) n -> p j n", p=P)).then_inc(w1_loaded[1], 16)
                elif s[0] == "xt" and s[2] == 0 and s[1] % 3 < 2:
                    for b in range(2 * n_win, 2 * n_win + 2):
                        sp.dma_start(sk_win[b, 0:512 - TQ, :], ck_win[b, TQ:512, :]).then_inc(win_out, 16)
                        sp.dma_start(sv_win[b, 0:512 - TQ, :], cv_win[b, TQ:512, :]).then_inc(win_out, 16)
                    n_win += 1
                elif s[0] == "load_wp":
                    n = s[1]
                    if n < 2:
                        sp.wait_ge(pt_used, len(PT_AT))
                    else:
                        sp.wait_ge(main_done, MAIN_AT[("main", "wp", n - 2, 3, 1)] + 1)
                    w, c0 = (w_pb if n % 2 else w_pa), n // 2 * 512
                    if n % 2:
                        sp.dma_start(wp[:, n % 2], w.rearrange("(k p) n -> p k n", p=P)[:, :, c0:c0 + 512])\
                            .then_inc(wp_loaded[n % 2], 32)
                    else:
                        for g in range(G):
                            sp.dma_start(wp[64 * g:64 * g + 64, n % 2],
                                         w.rearrange("(g k d) n -> g d k n", g=G, k=J)[g, :, :, c0:c0 + 512])\
                                .then_inc(wp_loaded[n % 2], 16)
                elif s[0] == "load_x":
                    sp.wait_ge(main_done, MAIN_AT[("main", "wp", 3, 3, 1)] + 1)
                    sp.wait_ge(m_lo, 16)
                    sp.dma_start(xr[96:128, NT, :], x_s).then_inc(xr_loaded, 16)
                    for i in range(NT):
                        sp.dma_start(xr[:, i, :], x_p[tok(i), :]).then_inc(xr_loaded, 16)
                    sp.dma_start(pm("norm_g"), final_g).then_inc(xr_loaded, 16)
                elif s[0] == "fin":
                    i = s[1]
                    sp.wait_ge(f_out, [4, 0, 1, 2, 3].index(i) + 1)
                    if i < NT:
                        sp.dma_start(y_p[tok(i), :], xr[:, i, :]).then_inc(y_out, 16)
                    else:
                        sp.dma_start(y_s, xr[96:128, NT, :]).then_inc(y_out, 16)
            sp.wait_ge(y_out, 16 * 5)
            sp.wait_ge(win_out, 16 * 2 * NB)
            sp.wait_ge(out_done, 16 * N_OUT)
            sp.wait_ge(cmp_out, 32)

        @block.gpsimd
        def _(pool):
            pool.memset(k_pad[:, :, :, :], 0.0).then_inc(pads_zero, 1)
            pool.memset(q_bd[:, :, :], 0.0).then_inc(pads_zero, 1)
            pool.memset(kcp[:, :, :], 0.0).then_inc(pads_zero, 1)
            pool.memset(st[:, 64:80], 0.0).then_inc(pads_zero, 1)
            pool.wait_ge(small_loaded, 32)
            pool.affine_select(out=ws_raw, in_=ws_raw, compare_op=ALU.is_ge, fill=0.0, base=0,
                               pattern=[[0, 4], [-1, P]], channel_multiplier=1).then_inc(ws_masked, 1)
            steps = [0]

            def rope(x, cos, sin, a, b):
                pool.tensor_tensor(a, x, cos, ALU.mult).then_inc(rope_step, 1)
                pool.tensor_tensor(b, x, sin, ALU.mult).then_inc(rope_step, 1)
                steps[0] += 2
                pool.wait_ge(rope_step, steps[0])
                nd = len(a.shape)
                lo, hi = (slice(None),) * (nd - 1) + (slice(0, 8),), (slice(None),) * (nd - 1) + (slice(8, 16),)
                pool.tensor_tensor(x[lo], a[lo], b[hi], ALU.subtract).then_inc(rope_step, 1)
                pool.tensor_tensor(x[hi], a[hi], b[lo], ALU.add).then_inc(rope_step, 1)
                steps[0] += 2
                pool.wait_ge(rope_step, steps[0])

            def rope_all(c0, heads):
                cos = cs("cos_tok").rearrange("p (i r) -> p i r", i=5)
                sin = cs("sin_tok").rearrange("p (i r) -> p i r", i=5)
                for rows, i0, i1 in [(P, 0, 2), (P, 2, 4), (TS, NT, NT + 1)]:
                    n = i1 - i0
                    for h0 in range(0, heads, 4):
                        hn = min(4, heads - h0)
                        a, b = (rt[0:rows, o:o + n * hn * ROT].rearrange("p (i h r) -> p i h r", i=n, h=hn) for o in (0, 256))
                        x = kq[0:rows, i0:i1, c0 + h0 * DH:c0 + (h0 + hn) * DH].rearrange("p i (h d) -> p i h d", h=hn)[:, :, :, 0:ROT]
                        shape = [rows, n, hn, ROT]
                        rope(x, cos[0:rows, i0:i1, :].unsqueeze(2).broadcast_to(shape),
                             sin[0:rows, i0:i1, :].unsqueeze(2).broadcast_to(shape), a, b)

            def store(dst_p, dst_s, src_p, src_s, done):
                pool.dma_start(dst_p.rearrange("(i p) c -> p i c", p=P), src_p).then_inc(done, 16)
                pool.dma_start(dst_s, src_s).then_inc(out_done, 16)

            def load(n):
                w, b = LOADS[n]
                if n >= RING:
                    if LOADS[n - RING][0] in ("kc", "vc"):
                        pool.wait_ge(repacked, n - RING + 1)
                    else:
                        pool.wait_ge(t_done, load_freed(n))
                slot, done = ring[:, n % RING, :], ring_loaded[n % RING]
                if b == "p":
                    src = pk_cmp if w == "kc" else pv_cmp
                    pool.dma_start(ring[0:64, n % RING, :], src.rearrange("(m r) c -> m (r c)", r=8)).then_inc(done, 16)
                elif w == "kw":
                    pool.dma_start(ring[:, n % RING, 0:512], ck_win[b].rearrange("(m r) c -> m (r c)", r=4)).then_inc(done, 16)
                else:
                    src = {"kc": ck_cmp, "vc": cv_cmp, "ks": ck_sel}[w]
                    pool.indirect_dma_start(slot, None, src, bass.IndirectOffsetOnAxis(rows_sb[:, b:b + 1], 0)).then_inc(done, 16)

            loaded = [0]

            def load_upto(n):
                while loaded[0] < min(n, len(LOADS)):
                    load(loaded[0])
                    loaded[0] += 1

            new_rows = lambda d: d[:, 512 - TQ:512, :]
            for s in ORDER:
                if s == ("out_cmp",):
                    wait_main_read(pool, last_of("B0"))
                    store(pk_cmp, sk_cmp, kq[:, 0:NT, 256:384], kq[0:TS, NT, 256:384], cmp_out)
                    store(pv_cmp, sv_cmp, kq[:, 0:NT, 384:512], kq[0:TS, NT, 384:512], cmp_out)
                    pool.wait_ge(rows_ready, 1)
                    load_upto(RING)
                elif s[0] == "rope":
                    if s[1] < 2:
                        wait_main_read(pool, last_of("B1" if s[1] == 0 else "C0"))
                        rope_all(128 * s[1], G)
                        c0 = 128 * s[1]
                        if s[1] == 0:
                            store(pk_sel, sk_sel, kq[:, 0:NT, c0:c0 + 128], kq[0:TS, NT, c0:c0 + 128], out_done)
                            store(pv_sel, sv_sel, v_tok[:, 0, 0:NT, :], v_tok[0:TS, 0, NT, :], out_done)
                        else:
                            store(pk_win, new_rows(sk_win), kq[:, 0:NT, c0:c0 + 128], kq[0:TS, NT, c0:c0 + 128], out_done)
                            store(pv_win, new_rows(sv_win), v_tok[:, 1, 0:NT, :], v_tok[0:TS, 1, NT, :], out_done)
                    else:
                        wait_main_read(pool, last_of("A1"))
                        rope_all(512, H)
                elif s == ("ln",):
                    pool.wait_ge(vn_ready, NT + 1)
                    pool.dma_start(s_chunk, vg[0:TS, NT, :]).then_inc(out_done, 16)
                elif s[0] == "xt" and s[2] % 2 == 0:
                    w, c = part(s[1])
                    n = LOAD_AT[(w, "p" if c == 2 else c * QB + s[2] // 2)]
                    if n == 0:
                        pool.wait_ge(cmp_out, 32)
                    rows = P if c < 2 else 64
                    pool.wait_ge(ring_loaded[n % RING], 16 * (n // RING + 1))
                    if n >= 2:
                        pool.wait_ge(t_done, packed_used(n - 2))
                    for g in range(G):
                        ins = pool.tensor_copy(packed[0:rows, n % 2, :].rearrange("p (q g r d) -> p q g r d", q=4, g=G, r=2)[:, :, g],
                                               ring[0:rows, n % RING, :].rearrange("p (q r g d) -> p q r g d", q=4, r=2, g=G)[:, :, :, g, :])
                    ins.then_inc(repacked, 1)
                    load_upto(n + RING + 1)
                elif s[0] == "qkT":
                    b = s[1]
                    if b % QB == 0:
                        if b == 0:
                            pool.wait_ge(hid_sum, 10)
                            pool.wait_ge(kc_done, 6)
                            pool.wait_ge(kc_ready, 6)
                        else:
                            pool.wait_ge(o_done, b // QB)
                        for n in range(QB):
                            pool.indirect_dma_start(U[:, n * 1024:n * 1024 + 1024], None, cv_sel,
                                                    bass.IndirectOffsetOnAxis(rows_sb[:, b + n:b + n + 1], 0)).then_inc(v_loaded, 16)
                            pool.dma_start(U[:, 4096 + n * 512:4608 + n * 512],
                                           cv_win[b + n].rearrange("(m r) c -> m (r c)", r=4)).then_inc(v_loaded, 16)
                    load_upto(LOAD_AT[("ks", b)] + RING + 1)

        @block.scalar
        def _(act):
            for s in ORDER:
                kind = s[0]
                t = T_AT[s]
                if kind == "norm":
                    act.wait_ge(x_loaded, 16 * 5)
                    act.wait_ge(st_ready, 1)
                    for i in range(NT + 1):
                        r = n_sp(i)
                        if i:
                            act.wait_ge(ssq_ready, i)
                        nc.scalar.activation(junk[0:r, :], x_in[0:r, i, :], ACT.Square,
                                             accum_out=st[0:r, i:i + 1]).then_inc(ssq_ready, 1)
                    act.wait_ge(root_in, 1)
                    nc.scalar.activation(st[:, 5:10], st[:, 5:10], ACT.Sqrt).then_inc(root_done, 1)
                elif kind == "split":
                    _, sl, hf = s
                    r, w = 2 * sl + hf, SLOTS[sl][3]
                    act.wait_ge(raw_loaded[r % NRAW], raw_count(r))
                    if sl >= 2:
                        act.wait_ge(main_done, slot_used(sl - 2))
                    for hi, lo, x in split_parts(sl, hf, r % NRAW, w):
                        ins = nc.scalar.copy(hi, x)
                    ins.then_inc(hi_done, 1)
                elif kind == "hT":
                    i = s[1]
                    n = n_sp(i)
                    for hf in range(2):
                        act.wait_ge(t_done, t + hf + 1)
                        nc.scalar.copy(h_hi[:, 4 * hf:4 * hf + 4, tok(i)],
                                       TB[(t + hf) % 2][:, 0:4 * n].rearrange("p (k n) -> p k n", k=4)).then_inc(hT_hi, 1)
                elif kind == "main" and s[1] != "wp":
                    name, mk = SLOTS[s[1]][0], SLOTS[s[1]][1]
                    n = MAIN_AT[s]
                    if mk == "wo":
                        continue
                    act.wait_ge(main_done, n + 1)
                    m = M[n % 2]
                    if mk == "tm":
                        i = s[2]
                        r = n_sp(i)
                        src = m[0:P, :] if i < NT else m[96:128, :]
                        if name == "B0":
                            nc.scalar.copy(kq[0:r, i, 256:512], src[:, 0:256]).then_inc(main_act, 1)
                        elif name == "B1":
                            nc.scalar.copy(kq[0:r, i, 0:128], src[:, 0:128])
                            nc.scalar.copy(v_tok[0:r, 0, i, :], src[:, 128:256]).then_inc(main_act, 1)
                        elif name == "C0":
                            nc.scalar.copy(kq[0:r, i, 128:256], src[:, 0:128])
                            nc.scalar.copy(v_tok[0:r, 1, i, :], src[:, 128:256])
                            nc.scalar.copy(gate[0:r, i, :], src[:, 256:280]).then_inc(main_act, 1)
                        elif name[0] == "A":
                            g = int(name[1])
                            nc.scalar.copy(kq[0:r, i, 512:1024].rearrange("p (j g d) -> p j g d", j=J, g=G)[:, :, g, :],
                                           src[:, 0:256].rearrange("p (j d) -> p j d", j=J)).then_inc(main_act, 1)
                        else:
                            c0 = 256 * int(name[1])
                            nc.scalar.activation(vg[0:r, i, c0:c0 + 256], src[:, 0:256], ACT.Gelu_apprx_tanh)\
                                .then_inc(main_act, 1)
                    elif name[0] == "U":
                        k = FN_AT[s]
                        if k >= 2:
                            act.wait_ge(mix_fn, k - 1)
                        nc.scalar.activation(tmp[:, k % 2, :], m[:, 0:HALF], ACT.Gelu_apprx_tanh).then_inc(main_act, 1)
                    elif name[0] == "Z":
                        k = FN_AT[s]
                        wait_tmp_read(act, k - 2)
                        nc.scalar.activation(tmp[:, k % 2, :], m[:, 0:HALF], ACT.Tanh, scale=0.5).then_inc(act_fn, 1)
                    else:
                        d = 2 * int(name[2]) + s[2]
                        nc.scalar.activation(sig_at(int(name[1] == "B"), d)[:, s[3] * HALF:(s[3] + 1) * HALF], m[:, 0:HALF],
                                             ACT.Tanh, scale=0.5).then_inc(main_act, 1)
                elif kind == "gates":
                    wait_main_read(act, last_of("C0"))
                    nc.scalar.activation(gate[:, 0:NT, :], gate[:, 0:NT, :], ACT.Tanh, scale=0.5)
                    nc.scalar.activation(gate[0:TS, NT, :], gate[0:TS, NT, :], ACT.Tanh, scale=0.5).then_inc(gl_tanh, 1)
                elif kind == "qT":
                    i = s[1]
                    act.wait_ge(t_done, t + 1)
                    nc.scalar.copy(qT[:, :, tok(i)], TB[t % 2][:, :].rearrange("p (j n) -> p j n", j=J)).then_inc(t_act, 1)
                elif kind == "ln":
                    act.wait_ge(var_ready, 1)
                    nc.scalar.activation(st[:, 20:25], st[:, 20:25], ACT.Sqrt).then_inc(std_ready, 1)
                elif kind == "xt" and T_USE[t] == "act":
                    c, n = s[1], s[2]
                    act.wait_ge(t_done, t + 1)
                    b, g = divmod(n, 2)
                    if n == 1 and c:
                        act.wait_ge(hid_sum, hid_count(c))
                    if n == 1 and c == 0:
                        act.wait_ge(out_done, 16 * (N_OUT - 1))
                        act.wait_ge(cmp_out, 32)
                    nc.scalar.copy(xt[:, :, g, b * P:(b + 1) * P],
                                   TB[t % 2][:, :].rearrange("p (q m) -> p q m", q=4)).then_inc(t_act, 1)
                elif kind == "hid":
                    c = s[1]
                    b1 = pm("b1k" if c < 3 else "b1v")
                    if c:
                        act.wait_ge(kc_done, c)
                    else:
                        act.wait_ge(rope_step, ROPE_STEPS[2])
                    if c % 3 < 2:
                        for g in range(G):
                            act.wait_ge(hid_sum, hid_count(c) + g + 1)
                            nc.scalar.activation(hid[:, g, :], S[g][:, 0:252], ACT.Gelu_apprx_tanh, bias=b1).then_inc(hid_ready, 1)
                    else:
                        act.wait_ge(hid_sum, hid_count(c) + 1)
                        nc.scalar.activation(hid[:, 0, 0:2 * NCP], S[0][:, 0:2 * NCP], ACT.Gelu_apprx_tanh, bias=b1).then_inc(hid_ready, 1)
                elif kind == "qkT":
                    b = s[1]
                    for k, dst in ((0, kt_s[:, 0:512]), (2, kt_w)):
                        act.wait_ge(t_done, t + k + 1)
                        if b:
                            act.wait_ge(qk_done, b)
                        else:
                            act.wait_ge(out_done, 16 * N_OUT)
                        nc.scalar.copy(dst, TB[(t + k) % 2][:, :]).then_inc(t_act, 1)
                elif kind == "s_max":
                    q = s[1]
                    act.wait_ge(s_bias, q + 1)
                    nc.scalar.activation(ps[:, CMP:CMP + NCS], O[:, 0:NCS], ACT.Exp, bias=st[:, 31:32], scale=SCALE,
                                         accum_out=st[:, 32:33]).then_inc(s_cexp, 1)
                elif kind == "s_exp":
                    q = s[1]
                    act.wait_ge(s_bias2, q + 1)
                    nc.scalar.activation(ps[:, 0:1056], ps[:, 0:1056], ACT.Exp, bias=st[:, 46:47], scale=SCALE,
                                         accum_out=st[:, 48:49])
                    nc.scalar.activation(ps[:, WIN:WIN + 512], S[2][:, :], ACT.Exp, bias=st[:, 47:48], scale=SCALE,
                                         accum_out=st[:, 49:50])
                    nc.scalar.activation(ps[:, WIN + 512:WIN + 544], ps[:, WIN + 512:WIN + 544], ACT.Exp, bias=st[:, 47:48],
                                         scale=SCALE, accum_out=st[:, 50:51]).then_inc(s_exp, 1)
                elif kind == "s_pv":
                    for k in (1, 3):
                        act.wait_ge(t_done, t + k + 1)
                        dst = ptr[1]
                        if k == 3:
                            act.wait_ge(pv_part, 2 * s[1] + 1)
                        nc.scalar.copy(dst, TB[(t + k) % 2][:, :]).then_inc(t_act, 1)
                elif kind == "cs":
                    act.wait_ge(c_in, s[1] + 1)
                    nc.scalar.activation(cp, cp, ACT.Exp, scale=SCALE).then_inc(c_exp, 1)
                elif kind in ("ct", "pt") and T_AT[s] < len(T_USE) and t_uses(s) == ["act"]:
                    act.wait_ge(t_done, t + 1)
                    r = PT_AT[s]
                    if r >= NPT:
                        act.wait_ge(pt_used, r - NPT + 1)
                    rows = NCP if kind == "ct" else P
                    nc.scalar.copy(ptb[0:rows, r % NPT, :], TB[t % 2][0:rows, :]).then_inc(t_act, 1)
                elif kind == "ps":
                    u = s[1]
                    n = (UNITS[u][0] + 1) * P
                    act.wait_ge(p_bias, u + 1)
                    m = 80 + 20 * (u % 2)
                    for j in range(J):
                        ins = nc.scalar.activation(pb[:, u % 2, j, 0:n], pb[:, u % 2, j, 0:n], ACT.Exp, bias=st[:, m + 4 + j:m + 5 + j],
                                                   scale=SCALE, accum_out=st[:, m + 8 + j:m + 9 + j])
                    ins.then_inc(p_exp, 1)
                elif kind == "main" and s[1] == "wp" and s[2] % 2:
                    n, d, hf = s[2:]
                    k = 2 * (n // 2 * 4 + d) + hf
                    act.wait_ge(m_sum, k + 1)
                    c = slice(hf * HALF, (hf + 1) * HALF)
                    nc.scalar.copy(h_hi[:, n // 2 * 4 + d, c], sig_at(0, n // 2 * 4 + d)[:, c]).then_inc(m_hi, 1)
                elif kind == "fin":
                    i = s[1]
                    k = [4, 0, 1, 2, 3].index(i)
                    r = slice(0, P) if i < NT else slice(96, 128)
                    wait_main_read(act, ("main", SLOT["WO3"], i, 0))
                    nc.scalar.activation(U[r, 5120:6144], xr[r, i, :], ACT.Square, accum_out=st[r, i:i + 1]).then_inc(f_ssq, 1)
                    act.wait_ge(f_ms, k + 1)
                    nc.scalar.activation(st[r, 5 + i:6 + i], st[r, 5 + i:6 + i], ACT.Sqrt).then_inc(f_root, 1)

        @block.vector
        def _(dve):
            v = nc.vector
            steps = [0]

            def seq(ins):
                steps[0] += 1
                ins.then_inc(dve_step, 1)
                dve.wait_ge(dve_step, steps[0])

            for s in ORDER:
                kind = s[0]
                t = T_AT[s]
                if kind == "norm":
                    v.memset(st[:, 0:30], 1.0).then_inc(st_ready, 1)
                    dve.wait_ge(small_loaded, 32)
                    dve.wait_ge(const_loaded, 32)
                    v.tensor_scalar(rows_sb[:, :], pages_sb[:, :], 16.0, cs("group_mod"), ALU.mult, ALU.add).then_inc(rows_ready, 1)
                    dve.wait_ge(ssq_ready, NT + 1)
                    v.tensor_scalar(st[:, 5:10], st[:, 0:5], 1.0 / D, EPS, ALU.mult, ALU.add).then_inc(root_in, 1)
                    dve.wait_ge(root_done, 1)
                    seq(v.reciprocal(st[:, 10:15], st[:, 5:10]))
                    for i in range(NT + 1):
                        r = n_sp(i)
                        v.scalar_tensor_tensor(x_in[0:r, i, :], x_in[0:r, i, :], st[0:r, 10 + i:11 + i], pm("norm_g", r),
                                               ALU.mult, ALU.mult).then_inc(h_ready, 1)
                elif kind == "split":
                    _, sl, hf = s
                    r, w = 2 * sl + hf, SLOTS[sl][3]
                    dve.wait_ge(hi_done, r + 1)
                    for hi, lo, x in split_parts(sl, hf, r % NRAW, w):
                        ins = v.tensor_tensor(lo, x, hi.bitcast(F32), ALU.subtract)
                    ins.then_inc(lo_done, 1)
                elif kind == "hT":
                    i = s[1]
                    n = n_sp(i)
                    for hf in range(2):
                        dve.wait_ge(hT_hi, 2 * i + hf + 1)
                        v.tensor_tensor(h_lo[:, 4 * hf:4 * hf + 4, tok(i)],
                                        TB[(t + hf) % 2][:, 0:4 * n].rearrange("p (k n) -> p k n", k=4),
                                        h_hi[:, 4 * hf:4 * hf + 4, tok(i)].bitcast(F32), ALU.subtract).then_inc(t_dve, 1)
                elif kind == "wsT":
                    dve.wait_ge(t_done, t + 1)
                    v.tensor_copy(wsT[:, :, :], TB[t % 2][:, :].rearrange("p (g n) -> p g n", g=4)).then_inc(t_dve, 1)
                elif kind == "wbd":
                    dve.wait_ge(t_done, t + 1)
                    same = cs("same_batch", TS).rearrange("p (b t) -> p b t", b=NB)
                    for g in range(4):
                        ins = v.tensor_tensor(w_bd[:, g, :].rearrange("p (b t) -> p b t", b=NB),
                                              TB[t % 2][0:TS, 4 * g:4 * g + 4].unsqueeze(1).broadcast_to([TS, NB, TQ]), same, ALU.mult)
                    ins.then_inc(t_dve, 1)
                elif kind == "kT":
                    y = s[1]
                    dve.wait_ge(pads_zero, 4)
                    dve.wait_ge(t_done, t + 1)
                    for g in range(G):
                        ins = v.tensor_copy(k_pad[64 * g:64 * g + 64, y, g, :], TB[t % 2][64 * g:64 * g + 64, :])
                    ins.then_inc(t_dve, 1)
                elif kind == "kTs":
                    dve.wait_ge(t_done, t + 1)
                    v.tensor_copy(k_newT[:, :, :], TB[t % 2][:, 0:2 * TS].rearrange("p (y n) -> p y n", y=2)).then_inc(t_dve, 1)
                elif kind == "qTs":
                    dve.wait_ge(t_done, t + 1)
                    for g in range(G):
                        for j in range(J):
                            ins = v.tensor_copy(q_bd[64 * g:64 * g + 64, :, (g * J + j) * TQ:(g * J + j + 1) * TQ],
                                                TB[t % 2][64 * g:64 * g + 64, j * TS:(j + 1) * TS].rearrange("p (b t) -> p b t", b=NB))
                    ins.then_inc(t_dve, 1)
                elif kind == "gates":
                    dve.wait_ge(gl_tanh, 1)
                    v.tensor_scalar(gate[:, 0:NT, :], gate[:, 0:NT, :], 0.5, 0.5, ALU.mult, ALU.add)
                    v.tensor_scalar(gate[0:TS, NT, :], gate[0:TS, NT, :], 0.5, 0.5, ALU.mult, ALU.add).then_inc(gate_ready, 1)
                    dve.wait_ge(gate_ready, 1)
                elif kind == "gr":
                    dve.wait_ge(t_done, t + 1)
                    for q in range(NQ):
                        seq(v.tensor_tensor(tmp[:, 0, 24 * q:24 * q + 24].rearrange("p (r h) -> p r h", r=3),
                                            TB[t % 2][:, 24 * q:24 * q + 24].rearrange("p (h r) -> p r h", r=3),
                                            cs("pick_head").unsqueeze(1).broadcast_to([P, 3, H]), ALU.mult))
                    v.tensor_reduce(gate_row[:, :, :], tmp[:, 0, 0:48].rearrange("p (q r h) -> p q r h", q=NQ, r=3), AX, ALU.add)\
                        .then_inc(t_dve, 1)
                elif kind == "ln":
                    for i in range(NT + 1):
                        r = n_sp(i)
                        if i == 0:
                            wait_main_read(dve, last_of("V1"))
                        seq(v.bn_stats(st[0:r, 100:106], vg[0:r, i, :]))
                        seq(v.bn_aggr(st[0:r, 106:108], st[0:r, 100:106]))
                        seq(v.tensor_copy(st[0:r, 15 + i:16 + i], st[0:r, 106:107]))
                        ins = v.tensor_scalar(st[0:r, 20 + i:21 + i], st[0:r, 107:108], EPS, None, ALU.add)
                    ins.then_inc(var_ready, 1)
                    dve.wait_ge(std_ready, 1)
                    seq(v.reciprocal(st[:, 25:30], st[:, 20:25]))
                    for i in range(NT + 1):
                        r = n_sp(i)
                        x = vg[0:r, i, :]
                        seq(v.tensor_scalar(x, x, st[0:r, 15 + i:16 + i], st[0:r, 25 + i:26 + i], ALU.subtract, ALU.mult))
                        seq(v.tensor_tensor(x, x, pm("v_g", r), ALU.mult))
                        v.tensor_tensor(x, x, pm("v_b", r), ALU.add).then_inc(vn_ready, 1)
                elif kind == "sp":
                    i = s[1]
                    dve.wait_ge(t_done, t + 1)
                    if i < NT:
                        v.tensor_tensor(sg[:, :, tok(i)], TB[t % 2][:, :].rearrange("p (g n) -> p g n", g=4),
                                        pm("b_sp").rearrange("p (g n) -> p g n", g=4), ALU.add).then_inc(t_dve, 1)
                    else:
                        for g in range(4):
                            ins = v.tensor_tensor(sg[:, g, TP:T].rearrange("p (b t) -> p b t", b=NB),
                                                  TB[t % 2][:, g * TS:(g + 1) * TS].rearrange("p (b t) -> p b t", b=NB),
                                                  pm("b_sp")[:, g * P:g * P + TQ].unsqueeze(1).broadcast_to([P, NB, TQ]), ALU.add)
                        ins.then_inc(t_dve, 1)
                elif kind == "main" and s[1] != "wp" and SLOTS[s[1]][0][0] in "UZ":
                    name, n, k = SLOTS[s[1]][0], MAIN_AT[s], FN_AT[s]
                    a, hf = s[2], s[3]
                    c = slice(hf * HALF, (hf + 1) * HALF)
                    f = tmp[:, k % 2, :]
                    if name[0] == "U":
                        wait_main_read(dve, s)
                        x = sg[:, 2 * int(name[1]) + a, c]
                        if k == 0:
                            wait_evacuated(dve, T_AT[("sp", NT)])
                        v.tensor_tensor(x, x, f, ALU.mult).then_inc(mix_fn, 1)
                    else:
                        dve.wait_ge(act_fn, k - 8 + 1)
                        tile = 2 * int(name[2]) + a
                        if name[1] == "A":
                            v.scalar_tensor_tensor(za[:, tile, c], f, 1.0, M[n % 2][:, 0:HALF], ALU.add, ALU.mult).then_inc(main_dve, 1)
                        else:
                            v.scalar_tensor_tensor(f, f, 1.0, M[n % 2][:, 0:HALF], ALU.add, ALU.mult).then_inc(main_dve, 1)
                            wait_main_read(dve, s)
                            v.scalar_tensor_tensor(sg[:, tile, c], sg[:, tile, c], 0.5, f, ALU.mult, ALU.mult).then_inc(mix_fn, 1)
                elif kind == "xt" and T_USE[t] == "dve":
                    c, n = s[1], s[2]
                    dve.wait_ge(t_done, t + 1)
                    if n == 0 and c:
                        dve.wait_ge(hid_sum, hid_count(c))
                    if c == 0 and n == 0:
                        dve.wait_ge(out_done, 16 * (N_OUT - 1))
                        dve.wait_ge(cmp_out, 32)
                    if c % 3 == 2:
                        v.tensor_copy(U[:, 0:512], TB[t % 2][:, :]).then_inc(t_dve, 1)
                    else:
                        b, g = divmod(n, 2)
                        v.tensor_copy(xt[:, :, g, b * P:(b + 1) * P],
                                      TB[t % 2][:, :].rearrange("p (q m) -> p q m", q=4)).then_inc(t_dve, 1)
                elif kind == "kc":
                    c = s[1]
                    dve.wait_ge(kc_done, c + 1)
                    if c < 3:
                        nb, nn = (QB, NCS) if c < 2 else (1, NCP)
                        for out, at, b2, tab in ((t1, 0, "b2k", "cos_blk"), (t2, 256, "b2kr", "sin_blk")):
                            seq(v.scalar_tensor_tensor(out[:, 0:nb * nn].rearrange("p (b n) -> p b n", b=nb),
                                                       S[2][:, at:at + nb * nn].rearrange("p (b n) -> p b n", b=nb), pm(b2),
                                                       cs(tab)[:, 0:nn].unsqueeze(1).broadcast_to([P, nb, nn]), ALU.add, ALU.mult))
                        if c < 2:
                            v.tensor_tensor(kcT[:, QB * c:QB * c + QB, :], t1.rearrange("p (b n) -> p b n", b=QB),
                                            t2.rearrange("p (b n) -> p b n", b=QB), ALU.add).then_inc(kc_ready, 1)
                        else:
                            for g in range(G):
                                r = slice(64 * g, 64 * g + 64)
                                ins = v.tensor_tensor(kcp[r, g, :], t1[r, 0:NCP], t2[r, 0:NCP], ALU.add)
                            ins.then_inc(kc_ready, 1)
                    elif c < 5:
                        v.tensor_tensor(vc[:, QB * (c - 3):QB * (c - 3) + QB, :], S[2][0:NCS, :].rearrange("p (b n) -> p b n", b=QB),
                                        pm("b2v", NCS).unsqueeze(1).broadcast_to([NCS, QB, P]), ALU.add).then_inc(kc_ready, 1)
                    else:
                        v.tensor_tensor(vcp[:, :], S[2][0:NCP, 0:P], pm("b2v", NCP), ALU.add).then_inc(kc_ready, 1)
                elif kind == "qkT":
                    b = s[1]
                    dve.wait_ge(t_done, t + 2)
                    if b:
                        dve.wait_ge(qk_done, b)
                    v.tensor_copy(kt_s[:, 512:1024], TB[(t + 1) % 2][:, :]).then_inc(t_dve, 1)
                elif kind == "s_max":
                    q = s[1]
                    dve.wait_ge(qk_done, QB * (q + 1))
                    seq(v.tensor_reduce(st[:, 30:31], O[:, 0:NCS], AX, ALU.max))
                    v.tensor_scalar(st[:, 31:32], st[:, 30:31], -SCALE, None, ALU.mult).then_inc(s_bias, 1)
                    dve.wait_ge(s_cexp, q + 1)
                    seq(v.reciprocal(st[:, 33:34], st[:, 32:33]))
                    v.tensor_scalar(ps[:, CMP:CMP + NCS], ps[:, CMP:CMP + NCS], st[:, 33:34], None, ALU.mult).then_inc(s_cp, 1)
                elif kind == "s_turn":
                    q = s[1]
                    dve.wait_ge(t_done, t + 1)
                    pj = pj_sum[0:NCS, 0:32]
                    v.tensor_reduce(pj.rearrange("p (b t) -> p b t", b=8),
                                    TB[t % 2][0:NCS, 0:P].rearrange("p (b j t) -> p b t j", b=8, j=J), AX, ALU.add).then_inc(t_dve, 1)
                    wait_evacuated(dve, t)
                    v.tensor_copy(pj_sum[0:NCS, 32:160].rearrange("p (b j t) -> p b j t", b=8, j=J),
                                  pj.rearrange("p (b t) -> p b t", b=8).unsqueeze(2).broadcast_to([NCS, 8, J, TQ])).then_inc(s_pj, 1)
                elif kind == "s_imp":
                    q = s[1]
                    dve.wait_ge(t_done, t + 1)
                    im = TB[t % 2][:, 1:15]
                    seq(v.tensor_reduce(st[:, 34:35], im, AX, ALU.min))
                    v.scalar_tensor_tensor(pick[:, 0:14], im, st[:, 34:35], cs("block_no"), ALU.is_le, ALU.mult).then_inc(t_dve, 1)
                    wait_evacuated(dve, t)
                    seq(v.tensor_reduce(st[:, 35:36], pick[:, 0:14], AX, ALU.max))
                    seq(v.tensor_scalar(st[:, 65:79], cs("block_no"), st[:, 35:36], NEG, ALU.is_equal, ALU.mult))
                    seq(v.tensor_copy(penalty.rearrange("p (n r) -> p n r", r=8), st[:, 64:80].unsqueeze(2).broadcast_to([P, 16, 8])))
                    nm = cs("new_mask")[:, q * TS:(q + 1) * TS]
                    for k in range(2):
                        v.tensor_tensor_reduce(ps[:, 512 * k:512 * k + 512].rearrange("p (s m) -> p s m", s=4),
                                               S[k][:, :].rearrange("p (s m) -> p s m", s=4),
                                               penalty.unsqueeze(1).broadcast_to([P, 4, P]), 1.0, -3e38, ALU.add, ALU.max,
                                               st[:, 40 + k:41 + k])
                    v.tensor_tensor_reduce(ps[:, 1024:1056], O[:, 64:96], nm, 1.0, -3e38, ALU.add, ALU.max, st[:, 42:43])
                    v.tensor_tensor_reduce(ps[:, WIN + 512:WIN + 544], O[:, 96:128], nm, 1.0, -3e38, ALU.add, ALU.max, st[:, 43:44])
                    early = S[2][:, 0:512:P]
                    seq(v.tensor_tensor(early, early, cs("win_mask"), ALU.add))
                    seq(v.tensor_reduce(st[:, 44:45], S[2][:, :], AX, ALU.max))
                    seq(v.tensor_reduce(st[:, 38:39], st[:, 40:43], AX, ALU.max))
                    seq(v.tensor_reduce(st[:, 39:40], st[:, 43:45], AX, ALU.max))
                    v.tensor_scalar(st[:, 46:48], st[:, 38:40], -SCALE, None, ALU.mult).then_inc(s_bias2, 1)
                elif kind == "s_scale":
                    q = s[1]
                    dve.wait_ge(s_exp, q + 1)
                    seq(v.tensor_tensor(st[:, 49:50], st[:, 49:50], st[:, 50:51], ALU.add))
                    seq(v.reciprocal(st[:, 36:38], st[:, 48:50]))
                    seq(v.tensor_tensor(st[:, 36:38], st[:, 36:38], gate_row[:, q, 1:3], ALU.mult))
                    v.tensor_scalar(ps[:, 0:1056], ps[:, 0:1056], st[:, 36:37], None, ALU.mult)
                    v.tensor_scalar(ps[:, WIN:WIN + 544], ps[:, WIN:WIN + 544], st[:, 37:38], None, ALU.mult)
                    v.tensor_scalar(ps[:, CMP:CMP + NCS], ps[:, CMP:CMP + NCS], gate_row[:, q, 0:1], None, ALU.mult).then_inc(s_p, 1)
                elif kind == "s_pv":
                    q = s[1]
                    dve.wait_ge(t_done, t + 1)
                    tb = TB[t % 2]
                    if q:
                        dve.wait_ge(o_done, q)
                    v.tensor_copy(pts[0:TS, 0:256], tb[0:TS, 0:256])
                    v.tensor_copy(pts[0:NCS, 256:384], tb[0:NCS, 256:384]).then_inc(t_dve, 1)
                    dve.wait_ge(t_done, t + 3)
                    v.tensor_copy(ptr[0], TB[(t + 2) % 2][:, :]).then_inc(t_dve, 1)
                elif kind == "s_out":
                    q = s[1]
                    dve.wait_ge(o_done, q + 1)
                    v.tensor_copy(o_row[:, :], O[:, 0:P]).then_inc(o_row_ready, 1)
                    dve.wait_ge(t_done, t + 1)
                    for g in range(G):
                        for j in range(J):
                            r = slice(64 * g, 64 * g + 64)
                            z = za[r, j, TP + 16 * q:TP + 16 * q + 16].rearrange("p (b t) -> p b t", b=QB)
                            o = TB[t % 2][r, 0:P].rearrange("p (b h t) -> p b h t", b=QB, h=H)[:, :, g * J + j, :]
                            ins = v.scalar_tensor_tensor(z, o, 0.5, z, ALU.mult, ALU.mult)
                    ins.then_inc(t_dve, 1)
                elif kind == "cs":
                    i = s[1]
                    dve.wait_ge(t_done, t + 1)
                    if i == 0:
                        dve.wait_ge(o_done, NQ)
                    else:
                        dve.wait_ge(t_done, T_AT[("ct", i - 1, 1)] + 1)
                    c3 = cp.rearrange("p (h n) -> p h n", h=H)
                    cm = cs("cmp_mask")[:, i * NCP:(i + 1) * NCP].unsqueeze(1).broadcast_to([P, H, NCP])
                    v.tensor_tensor(c3, TB[t % 2][:, 0:H * NCP].rearrange("p (h n) -> p h n", h=H), cm, ALU.add).then_inc(t_dve, 1)
                    wait_evacuated(dve, t)
                    seq(v.tensor_reduce(st[:, 0:8], c3, AX, ALU.max))
                    v.tensor_tensor(c3, c3, st[:, 0:8].unsqueeze(2).broadcast_to([P, H, NCP]), ALU.subtract).then_inc(c_in, 1)
                elif kind == "cn":
                    i = s[1]
                    c3 = cp.rearrange("p (h n) -> p h n", h=H)
                    dve.wait_ge(c_exp, i + 1)
                    seq(v.tensor_reduce(st[:, 8:16], c3, AX, ALU.add))
                    seq(v.reciprocal(st[:, 16:24], st[:, 8:16]))
                    gc = gate[:, i, :].rearrange("p (g j r) -> p j g r", g=G, j=J)[:, :, :, 0]
                    w = st[:, 16:24].rearrange("p (j g) -> p j g", j=J)
                    seq(v.tensor_tensor(w, w, gc, ALU.mult))
                    if i == 0:
                        seq(v.tensor_scalar(st[:, 16:24], st[:, 16:24], cs("row_mask"), None, ALU.mult))
                    v.tensor_tensor(c3, c3, st[:, 16:24].unsqueeze(2).broadcast_to([P, H, NCP]), ALU.mult).then_inc(c_p, 1)
                elif kind in ("ct", "pt") and t_uses(s) == ["dve"]:
                    dve.wait_ge(t_done, t + 1)
                    r = PT_AT[s]
                    if r >= NPT:
                        dve.wait_ge(pt_used, r - NPT + 1)
                    rows = NCP if kind == "ct" else P
                    v.tensor_copy(ptb[0:rows, r % NPT, :], TB[t % 2][0:rows, :]).then_inc(t_dve, 1)
                elif kind == "ps":
                    u = s[1]
                    i, g, y = UNITS[u]
                    n = (i + 1) * P
                    m = 80 + 20 * (u % 2)
                    if u < 2:
                        dve.wait_ge(o_done, NQ)
                    else:
                        dve.wait_ge(t_done, T_AT[("pt", u - 2, UNITS[u - 2][0])] + 1)
                    for j in range(J):
                        k = J * u + j
                        dve.wait_ge(p_scored, k + 1)
                        v.tensor_tensor_reduce(pb[:, u % 2, j, 0:n], S[k % 3][:, 0:n], cs("causal")[:, 512 - n:512], 1.0, -3e38,
                                               ALU.add, ALU.max, st[:, m + j:m + j + 1]).then_inc(p_masked, 1)
                    dve.wait_ge(p_masked, J * u + J)
                    v.tensor_scalar(st[:, m + 4:m + 8], st[:, m:m + 4], -SCALE, None, ALU.mult).then_inc(p_bias, 1)
                elif kind == "pn":
                    u = s[1]
                    i, g, y = UNITS[u]
                    n = (i + 1) * P
                    m = 80 + 20 * (u % 2)
                    dve.wait_ge(p_exp, u + 1)
                    seq(v.reciprocal(st[:, m + 12:m + 16], st[:, m + 8:m + 12]))
                    gy = gate[:, i, :].rearrange("p (g j r) -> p g j r", g=G, j=J)[:, g, :, y + 1]
                    seq(v.tensor_tensor(st[:, m + 12:m + 16], st[:, m + 12:m + 16], gy, ALU.mult))
                    for j in range(J):
                        ins = v.tensor_scalar(pb[:, u % 2, j, 0:n], pb[:, u % 2, j, 0:n], st[:, m + 12 + j:m + 13 + j], None, ALU.mult)
                    ins.then_inc(p_scaled, 1)
                elif kind == "oz":
                    i = s[1]
                    dve.wait_ge(pt_used, PT_AT[("pt", max(n for n, x in enumerate(UNITS) if x[0] == i), i)] + 1)
                    v.scalar_tensor_tensor(za[:, :, tok(i)], O[:, :].rearrange("p (j n) -> p j n", j=J), 0.5, za[:, :, tok(i)],
                                           ALU.mult, ALU.mult).then_inc(mix_ready, 1)
                elif kind == "main" and s[1] == "wp":
                    _, _, n, d, hf = s
                    dt = n // 2 * 4 + d
                    c = slice(hf * HALF, (hf + 1) * HALF)
                    m = MAIN_AT[s]
                    dve.wait_ge(main_done, m + 1)
                    if n == 0 and d == 0 and hf == 0:
                        wait_main_read(dve, ("main", SLOT["RB3"], 1, 1))
                    x = sig_at(n % 2, dt)[:, c]
                    v.scalar_tensor_tensor(x, x, 1.0, M[m % 2][:, 0:HALF], ALU.add, ALU.mult).then_inc(main_dve, 1)
                    if n % 2:
                        wait_main_read(dve, s)
                        a = sig_at(0, dt)[:, c]
                        v.tensor_tensor(a, a, x, ALU.add).then_inc(m_sum, 1)
                elif kind == "mlo":
                    _, dt, hf = s
                    c = slice(hf * HALF, (hf + 1) * HALF)
                    dve.wait_ge(m_hi, 2 * dt + hf + 1)
                    v.tensor_tensor(h_lo[:, dt, c], sig_at(0, dt)[:, c], h_hi[:, dt, c].bitcast(F32), ALU.subtract).then_inc(m_lo, 1)
                elif kind == "main" and SLOTS[s[1]][1] == "wo":
                    n, i, c = MAIN_AT[s], s[2], SLOTS[s[1]][2]
                    r = slice(0, P) if i < NT else slice(96, 128)
                    dve.wait_ge(main_done, n + 1)
                    if s == ("main", SLOT["WO0"], 4, 0):
                        dve.wait_ge(xr_loaded, 16 * 6)
                    x = xr[r, i, c:c + 256]
                    v.scalar_tensor_tensor(x, M[n % 2][r, 0:256], 0.5, x, ALU.mult, ALU.add).then_inc(main_dve, 1)
                elif kind == "fin":
                    i = s[1]
                    k = [4, 0, 1, 2, 3].index(i)
                    r = slice(0, P) if i < NT else slice(96, 128)
                    dve.wait_ge(f_ssq, k + 1)
                    v.tensor_scalar(st[r, 5 + i:6 + i], st[r, i:i + 1], 1.0 / D, EPS, ALU.mult, ALU.add).then_inc(f_ms, 1)
                    dve.wait_ge(f_root, k + 1)
                    seq(v.reciprocal(st[r, 10 + i:11 + i], st[r, 5 + i:6 + i]))
                    v.scalar_tensor_tensor(xr[r, i, :], xr[r, i, :], st[r, 10 + i:11 + i], pm("norm_g")[r], ALU.mult, ALU.mult)\
                        .then_inc(f_out, 1)

        @block.tensor
        def _(pe):
            mm = nc.tensor.matmul

            def passes(out, lhs, rhs, n):
                for k in range(n):
                    for a, b in ((0, 0), (0, 1), (1, 0)):
                        ins = mm(out, lhs(a, k), rhs(b, k), start=(k == 0 and a + b == 0), stop=(k == n - 1 and a == 1))
                return ins

            for s in ORDER:
                kind = s[0]
                t = T_AT[s]
                tb = TB[t % 2]
                if kind in ("xt",) or t_uses(s):
                    wait_t_bank(pe, t)
                if kind == "hT":
                    i = s[1]
                    n = n_sp(i)
                    pe.wait_ge(h_ready, i + 1)
                    if i == 0:
                        pe.wait_ge(const_loaded, 32)
                    for hf in range(2):
                        if hf:
                            wait_t_bank(pe, t + hf)
                        for k in range(4):
                            kk = 4 * hf + k
                            ins = pe.transpose(TB[(t + hf) % 2][:, k * n:(k + 1) * n], x_in[0:n, i, kk * P:(kk + 1) * P], ident[0:n, 0:n])
                        ins.then_inc(t_done, 1)
                elif kind == "wsT":
                    pe.wait_ge(ws_masked, 1)
                    for g in range(4):
                        ins = pe.transpose(tb[:, g * P:(g + 1) * P], ws_raw[:, g, :], ident)
                    ins.then_inc(t_done, 1)
                elif kind == "wbd":
                    wait_evacuated(pe, T_AT[("wsT",)])
                    mm(tb[0:TS, 0:16].rearrange("p (g t) -> p g t", g=4), cs("repeat4", TQ), wsT[0:TQ, :, 0:TQ], start=True, stop=True)\
                        .then_inc(t_done, 1)
                elif kind == "kT":
                    pe.wait_ge(rope_step, ROPE_STEPS[s[1]])
                    for i in range(NT):
                        ins = pe.transpose(tb[:, tok(i)], kq[:, i, 128 * s[1]:128 * s[1] + 128], ident)
                    ins.then_inc(t_done, 1)
                elif kind == "kTs":
                    for y in range(2):
                        ins = pe.transpose(tb[:, y * TS:(y + 1) * TS], kq[0:TS, NT, 128 * y:128 * y + 128], ident[0:TS, 0:TS])
                    ins.then_inc(t_done, 1)
                elif kind in ("qT", "qTs"):
                    i = s[1] if kind == "qT" else NT
                    n = n_sp(i)
                    pe.wait_ge(rope_step, ROPE_STEPS[2])
                    for j in range(J):
                        src = kq[0:n, i, 512 + j * P:512 + (j + 1) * P]
                        ins = pe.transpose(tb[:, j * n:(j + 1) * n], src, ident[0:n, 0:n])
                    ins.then_inc(t_done, 1)
                elif kind == "gr":
                    pe.wait_ge(gate_ready, 1)
                    for q in range(NQ):
                        ins = mm(tb[:, 24 * q:24 * q + 24], cs("pick_rows", TS)[:, q * P:(q + 1) * P], gate[0:TS, NT, :], start=True, stop=True)
                    ins.then_inc(t_done, 1)
                elif kind == "main":
                    n = MAIN_AT[s]
                    wait_main_bank(pe, n)
                    out = M[n % 2]
                    if s[1] == "wp":
                        _, _, w, d, hf = s
                        if d == 0 and hf == 0:
                            pe.wait_ge(wp_loaded[w % 2], 32 * (w // 2 + 1))
                            if w == 0:
                                pe.wait_ge(mix_ready, NT)
                                pe.wait_ge(mix_fn, 16)
                        x = sg if w % 2 else za
                        for k in range(4):
                            ins = mm(out[:, 0:HALF], wp[:, w % 2, k, d * P:(d + 1) * P], x[:, k, hf * HALF:(hf + 1) * HALF],
                                     start=(k == 0), stop=(k == 3))
                        ins.then_inc(main_done, 1)
                        continue
                    sl = s[1]
                    name, mk, _, w = SLOTS[sl]
                    pe.wait_ge(lo_done, 2 * sl + 2)
                    hx, wx = (h_hi, h_lo), (w_hi, w_lo)
                    if mk in ("tm", "wo"):
                        i = s[2]
                        if s == ("main", 0, 0, 0):
                            pe.wait_ge(t_dve, 10)
                        if mk == "wo":
                            pe.wait_ge(m_lo, 16)
                        c = tok(i) if i < NT else slice(T - P, T)
                        ins = passes(out[:, 0:w], lambda a, k: hx[a][:, k, c], lambda b, k: wx[b][:, sl % 2, k, 0:w], KD)
                    else:
                        a_, hf = s[2], s[3]
                        lhs = lambda a, k: wx[a][:, sl % 2, k, a_ * P:(a_ + 1) * P]
                        ins = passes(out[:, 0:HALF], lhs, lambda b, k: hx[b][:, k, hf * HALF:(hf + 1) * HALF], KD)
                    ins.then_inc(main_done, 1)
                elif kind == "sp":
                    i = s[1]
                    n = n_sp(i)
                    pe.wait_ge(vn_ready, i + 1)
                    if i == NT:
                        wait_evacuated(pe, T_AT[("wbd",)])
                    for g in range(4):
                        w = wsT[:, g, :] if i < NT else w_bd[:, g, :]
                        ins = mm(tb[:, g * n:(g + 1) * n], vg[0:n, i, g * P:(g + 1) * P], w, start=True, stop=True)
                    ins.then_inc(t_done, 1)
                elif kind == "xt":
                    c, n = s[1], s[2]
                    w, cc = part(c)
                    b, g = divmod(n, 2)
                    ld = LOAD_AT[(w, "p" if cc == 2 else cc * QB + b)]
                    pe.wait_ge(repacked, ld + 1)
                    if cc < 2:
                        for q in range(4):
                            ins = pe.transpose(tb[:, q * P:(q + 1) * P], packed[:, ld % 2, (2 * q + g) * P:(2 * q + g + 1) * P], ident)
                    else:
                        for k in range(8):
                            ins = pe.transpose(tb[:, k * 64:k * 64 + 64], packed[0:64, ld % 2, k * P:(k + 1) * P], ident[0:64, 0:64])
                    ins.then_inc(t_done, 1)
                elif kind == "hid":
                    c = s[1]
                    w, cc = part(c)
                    w1 = w1_at[c // 3]
                    pe.wait_ge(w1_loaded[c // 3], 16)
                    for k in range(8 if cc < 2 else 1):
                        if k >= (6 if cc < 2 else 0):
                            wait_evacuated(pe, T_AT[("xt", c, k)])
                    if c:
                        pe.wait_ge(hid_ready, hid_count(c))
                    for g in range(G if cc < 2 else 1):
                        for j in range(16):
                            o = j // 4
                            if cc < 2:
                                rhs = xt[:, j % 4, g, :].rearrange("p (b m) -> p b m", b=QB)[:, :, o:o + 2 * NCS - 1:2]
                                out = S[g][:, 0:252]
                            else:
                                rhs = xtp[:, j % 4, :, o:o + 2 * NCP - 1:2]
                                out = S[0][:, 0:2 * NCP]
                            ins = mm(out, w1[:, j, :], rhs, start=(j == 0), stop=(j == 15))
                        ins.then_inc(hid_sum, 1)
                elif kind == "kc":
                    c = s[1]
                    pe.wait_ge(hid_ready, hid_count(c + 1))
                    if c:
                        pe.wait_ge(kc_ready, c)
                    if c < 3:
                        n = 252 if c < 2 else NCP
                        for g in range(G):
                            x = hid[:, g, :] if c < 2 else hid[:, 0, g * NCP:(g + 1) * NCP]
                            for k, w2 in enumerate(("w2k", "w2kr")):
                                ins = mm(S[2][64 * g:64 * g + 64, 256 * k:256 * k + n], pm(w2), x, start=True, stop=True)
                    elif c < 5:
                        for b in range(QB):
                            for g in range(G):
                                ins = mm(S[2][0:NCS, b * P + g * DH:b * P + (g + 1) * DH], hid[:, g, b * NCS:(b + 1) * NCS], pm("w2v"),
                                         start=True, stop=True)
                    else:
                        for g in range(G):
                            ins = mm(S[2][0:NCP, g * DH:(g + 1) * DH], hid[:, 0, g * NCP:(g + 1) * NCP], pm("w2v"), start=True, stop=True)
                    ins.then_inc(kc_done, 1)
                elif kind == "qkT":
                    b = s[1]
                    for k in range(3):
                        ld = LOAD_AT[("ks" if k < 2 else "kw", b)]
                        if k != 1:
                            pe.wait_ge(ring_loaded[ld % RING], 16 * (ld // RING + 1))
                        if k:
                            wait_t_bank(pe, t + k)
                        for q in range(4):
                            x = ring[:, ld % RING, (4 * (k % 2) + q) * P:(4 * (k % 2) + q + 1) * P]
                            ins = pe.transpose(TB[(t + k) % 2][:, q * P:(q + 1) * P], x, ident)
                        ins.then_inc(t_done, 1)
                elif kind == "qkS":
                    b = s[1]
                    for k in range(3):
                        wait_evacuated(pe, T_AT[("qkT", b)] + k)
                    if b == 0:
                        pe.wait_ge(kc_ready, 6)
                        wait_evacuated(pe, T_AT[("qTs",)])
                        wait_evacuated(pe, T_AT[("kTs",)])
                    if b == QB:
                        pe.wait_ge(s_exp, 1)
                        pe.wait_ge(o_row_ready, 1)
                    r = slice(32 * (b % QB), 32 * (b % QB) + 32)
                    q = q_bd[:, b, :]
                    for k in range(2):
                        mm(S[k][r, :], q, kt_s[:, 512 * k:512 * k + 512], start=True, stop=True)
                    mm(S[2][r, :], q, kt_w, start=True, stop=True)
                    mm(O[r, 0:NCS], q, kcT[:, b, :], start=True, stop=True)
                    for y in range(2):
                        ins = mm(O[r, 64 + 32 * y:96 + 32 * y], q, k_newT[:, y, :], start=True, stop=True)
                    ins.then_inc(qk_done, 1)
                elif kind == "s_turn":
                    pe.wait_ge(s_cp, s[1] + 1)
                    pe.transpose(tb[0:NCS, 0:P], ps[:, CMP:CMP + NCS], ident).then_inc(t_done, 1)
                elif kind == "s_imp":
                    pe.wait_ge(s_pj, s[1] + 1)
                    mm(tb[:, 0:NSEL], pj_sum[0:NCS, 32:160], cs("overlap", NCS), start=True, stop=True).then_inc(t_done, 1)
                elif kind == "s_pv":
                    q = s[1]
                    pe.wait_ge(s_p, q + 1)
                    pe.transpose(tb[0:TS, 0:P], ps[:, 1024:1056], ident)
                    pe.transpose(tb[0:TS, P:2 * P], ps[:, WIN + 512:WIN + 544], ident)
                    pe.transpose(tb[0:NCS, 2 * P:3 * P], ps[:, CMP:CMP + NCS], ident).then_inc(t_done, 1)

                    def turn(k):
                        c0 = (0, 0, 512, WIN)[k]
                        wait_t_bank(pe, t + k)
                        for m in range(4):
                            ins = pe.transpose(TB[(t + k) % 2][:, m * P:(m + 1) * P], ps[:, c0 + m * P:c0 + (m + 1) * P], ident)
                        ins.then_inc(t_done, 1)

                    turn(1)
                    wait_evacuated(pe, t)
                    pe.wait_ge(v_loaded, 16 * 2 * QB * (q + 1))
                    for y in range(2):
                        mm(O[:, 0:P], pts[0:TS, y * P:(y + 1) * P], v_tok[0:TS, y, NT, :], start=(y == 0), stop=False, skip_group_check=True)
                    for b in range(QB):
                        mm(O[32 * b:32 * b + 32, 0:P], pts[0:NCS, 2 * P + 32 * b:2 * P + 32 * b + 32], vc[:, QB * q + b, :],
                           start=False, stop=False, skip_group_check=True)
                    for k in range(1, 4):
                        if k < 3:
                            turn(k + 1)
                        wait_evacuated(pe, t + k)
                        src = (None, ptr[1], ptr[0], ptr[1])[k]
                        for b in range(QB):
                            for m in range(4):
                                val = vs[:, b, 4 * (k - 1) + m, :] if k < 3 else vw[:, b, m, :]
                                ins = mm(O[32 * b:32 * b + 32, 0:P], src[:, m * P + 32 * b:m * P + 32 * b + 32], val,
                                         start=False, stop=(k == 3 and m == 3), skip_group_check=True)
                        ins.then_inc(pv_part if k < 3 else o_done, 1)
                elif kind == "s_out":
                    pe.wait_ge(o_row_ready, s[1] + 1)
                    pe.transpose(tb[:, 0:P], o_row[:, :], ident).then_inc(t_done, 1)
                elif kind == "cs":
                    i = s[1]
                    if i == 0:
                        wait_evacuated(pe, T_AT[("qT", NT - 1)])
                        wait_evacuated(pe, T_AT[("kT", 1)])
                    for j in range(J):
                        ins = mm(tb[:, j * 2 * NCP:(j + 1) * 2 * NCP].rearrange("p (g n) -> p g n", g=G), qT[:, j, tok(i)], kcp[:, :, :], start=True, stop=True)
                    ins.then_inc(t_done, 1)
                elif kind == "ct":
                    i, g = s[1], s[2]
                    pe.wait_ge(c_p, i + 1)
                    if g == 0 and i:
                        pe.wait_ge(mix_ready, i)
                    for j in range(J):
                        c0 = (j * G + g) * NCP
                        ins = pe.transpose(tb[0:NCP, j * P:(j + 1) * P], cp[:, c0:c0 + NCP], ident)
                    ins.then_inc(t_done, 1)
                    wait_evacuated(pe, t)
                    mm(O[64 * g:64 * g + 64, :], vcp[:, g * DH:(g + 1) * DH], ptb[0:NCP, PT_AT[s] % NPT, :], start=True, stop=False,
                       skip_group_check=True).then_inc(pt_used, 1)
                elif kind == "ps":
                    u = s[1]
                    i, g, y = UNITS[u]
                    n = (i + 1) * P
                    for j in range(J):
                        k = J * u + j
                        if k >= 3:
                            pe.wait_ge(p_masked, k - 2)
                        if k == 0:
                            pe.wait_ge(s_exp, NQ)
                        mm(S[k % 3][:, 0:n], qT[:, j, tok(i)], k_pad[:, y, g, 0:n], start=True, stop=True).then_inc(p_scored, 1)
                elif kind == "pt":
                    u, kt = s[1], s[2]
                    i, g, y = UNITS[u]
                    if kt <= i:
                        if kt == 0:
                            pe.wait_ge(p_scaled, u + 1)
                        for j in range(J):
                            ins = pe.transpose(tb[:, j * P:(j + 1) * P], pb[:, u % 2, j, kt * P:(kt + 1) * P], ident)
                        ins.then_inc(t_done, 1)
                    if kt:
                        k = kt - 1
                        wait_evacuated(pe, T_AT[("pt", u, k)])
                        ins = mm(O[64 * g:64 * g + 64, :], v_tok[:, y, k, g * DH:(g + 1) * DH], ptb[:, PT_AT[("pt", u, k)] % NPT, :],
                                 start=False, stop=(y == 1 and k == i), skip_group_check=True)
                        ins.then_inc(pt_used, 1)


OUTS = [("y_p", (TP, D)), ("y_s", (TS, D)), ("pk_cmp", (TP, P)), ("pv_cmp", (TP, P)), ("pk_sel", (TP, P)),
        ("pv_sel", (TP, P)), ("pk_win", (TP, P)), ("pv_win", (TP, P)), ("sk_cmp", (TS, P)), ("sv_cmp", (TS, P)),
        ("sk_sel", (TS, P)), ("sv_sel", (TS, P)), ("sk_win", (NB, 512, P)), ("sv_win", (NB, 512, P)), ("s_chunk", (TS, 512))]


def kernel(x_prompt, x_sample, cache_k_cmp, cache_v_cmp, cache_k_sel, cache_v_sel, cache_k_win, cache_v_win, page_table,
           norm_g, w_in, cmp_k_w1, cmp_k_b1, cmp_k_w2, cmp_k_b2, cmp_v_w1, cmp_v_b1, cmp_v_w2, cmp_v_b2,
           v_norm_g, v_norm_b, w_spatial, b_spatial, w_pa, w_pb, w_o, final_g):
    import concourse.bacc as bacc
    from concourse.bass_utils import run_bass_kernel_spmd

    A = np.asarray

    def rows(a, n=P):
        return np.ascontiguousarray(np.broadcast_to(A(a).reshape(1, -1), (n, A(a).size)))

    def turned(a):
        return np.concatenate([a[..., 8:16], a[..., 0:8], a[..., 16:]], -1)

    def column(a):
        return np.tile(A(a).reshape(-1, 1), (P // A(a).size, 1))

    params = np.zeros((P, N_PARAM), np.float32)
    for name, a in (("norm_g", rows(norm_g)), ("v_g", rows(v_norm_g)), ("v_b", rows(v_norm_b)), ("b_sp", rows(b_spatial)),
                    ("w2k", A(cmp_k_w2)[0]), ("w2kr", turned(A(cmp_k_w2)[0])), ("w2v", A(cmp_v_w2)[0]),
                    ("b1k", column(cmp_k_b1)), ("b1v", column(cmp_v_b1)), ("b2k", column(cmp_k_b2)),
                    ("b2kr", column(turned(A(cmp_k_b2)[0]))), ("b2v", rows(np.concatenate([A(cmp_v_b2)[0]] * 2)))):
        params[:, PARAMS[name][0]:PARAMS[name][1]] = a
    given = [
        ("x_p", A(x_prompt).reshape(TP, D)), ("x_s", A(x_sample).reshape(TS, D)),
        ("ck_cmp", A(cache_k_cmp).reshape(-1, 8 * P)), ("cv_cmp", A(cache_v_cmp).reshape(-1, 8 * P)),
        ("ck_sel", A(cache_k_sel).reshape(-1, 8 * P)), ("cv_sel", A(cache_v_sel).reshape(-1, 8 * P)),
        ("ck_win", A(cache_k_win).reshape(NB, 512, P)), ("cv_win", A(cache_v_win).reshape(NB, 512, P)),
        ("pages", np.repeat(A(page_table).T, P // (PAST // PAGE), axis=0)),
        ("w_in", A(w_in)[0]), ("w1k", A(cmp_k_w1)[0]), ("w1v", A(cmp_v_w1)[0]), ("w_sp", A(w_spatial)[0].transpose(1, 0, 2)),
        ("w_pa", A(w_pa)[0]), ("w_pb", A(w_pb)[0]), ("w_o", A(w_o)[0]), ("final_g", rows(final_g)),
        ("params", params), ("consts", constants()),
    ]
    nc = bacc.Bacc("TRN2", target_bir_lowering=False, num_devices=1)
    arrays, args = {}, []
    for name, a in given:
        a = np.ascontiguousarray(a)
        arrays["in_" + name] = a
        args.append(nc.dram_tensor("in_" + name, a.shape, mybir.dt.from_np(a.dtype), kind="ExternalInput").ap())
    outs = [nc.dram_tensor("out_" + name, shape, F32, kind="ExternalOutput").ap() for name, shape in OUTS]
    nsa_gmlp_layer(nc, *args, outs)
    r = run_bass_kernel_spmd(nc, [arrays], core_ids=[0]).results[0]
    got = {name: r["out_" + name] for name, _ in OUTS}
    heads = (G, DH)
    return (got["y_p"].reshape(1, TP, D), got["y_s"].reshape(NB, TQ, D),
            *(got[n].reshape(1, 1, TP, *heads) for n in ("pk_cmp", "pv_cmp", "pk_sel", "pv_sel", "pk_win", "pv_win")),
            *(got[n].reshape(1, NB, TQ, *heads) for n in ("sk_cmp", "sv_cmp", "sk_sel", "sv_sel")),
            *(got[n].reshape(1, NB, 512, *heads) for n in ("sk_win", "sv_win")),
            got["s_chunk"].reshape(1, NB, TQ, 512))
```

```python
from contextlib import ExitStack

import numpy as np
import concourse.bass as bass
from concourse import mybir

F32 = mybir.dt.float32
F32R = mybir.dt.float32r
I32 = mybir.dt.int32
U32 = mybir.dt.uint32
ALU = mybir.AluOpType
ACT = mybir.ActivationFunctionType
AX = mybir.AxisListType.X

P = 128
D = 1024
KD = D // P
TP, NB, TQ = 512, 8, 4
TS = NB * TQ
T = TP + TS
NT = TP // P
HALF = T // 2
G, J, H, DH = 2, 4, 8, 64
PAST, PAGE = 1024, 128
NCS = (PAST + TQ - 32) // 16 + 1
NCP = (TP - 32) // 16 + 1
NSEL = PAST // 64 + 1
QB = 4
NQ = NB // QB
NEG = -1e30
EPS = 1e-6
SCALE = DH ** -0.5
ROT = 16
THETA = 500000.0

C_Q, C_KCMP, C_KSEL, C_KWIN, C_GL, C_ZA, C_U, C_V, C_ZB, C_R = 0, 512, 768, 1024, 1280, 1304, 1816, 2328, 2840, 3352
SW = 280
SLOTS = [("B0", "tm", C_KCMP, 256), ("B1", "tm", C_KSEL, 256), ("C0", "tm", C_KWIN, 280),
         ("A0", "tm", C_Q, 256), ("A1", "tm", C_Q + 256, 256), ("V0", "tm", C_V, 256), ("V1", "tm", C_V + 256, 256),
         ("U0", "tr", C_U, 256), ("U1", "tr", C_U + 256, 256),
         ("ZA0", "tr", C_ZA, 256), ("ZA1", "tr", C_ZA, 256),
         ("ZB0", "tr", C_ZB, 256), ("ZB1", "tr", C_ZB + 256, 256)] + \
        [(f"RA{n}", "tr", C_R + 256 * n, 256) for n in range(4)] + \
        [(f"RB{n}", "tr", C_R + D + 256 * n, 256) for n in range(4)] + \
        [(f"P{n}", "wp", 256 * n, 256) for n in range(4)] + \
        [(f"WO{n}", "wo", 256 * n, 256) for n in range(4)]
SLOT = {s[0]: n for n, s in enumerate(SLOTS)}
NRAW = 3
LAST_TILES = [0, 1, 2, 3, 4]

FIN_CUT = 704

CONSTS = {}


def _layout(items):
    at = 0
    for name, width in items:
        CONSTS[name] = (at, at + width)
        at += width
    return at


NC_CONST = _layout([("ident", 128), ("causal", 512), ("cos_tok", 5 * ROT), ("sin_tok", 5 * ROT), ("cos_blk", NCS),
                    ("sin_blk", NCS), ("cmp_mask", NT * NCP), ("row_mask", 1), ("pick_rows", NQ * P),
                    ("pick_head", H), ("new_mask", NQ * TS), ("win_mask", TQ), ("overlap", NSEL), ("block_no", 14),
                    ("repeat4", TS), ("same_batch", TS), ("group_mod", 1)])


def constants():
    c = np.zeros((P, NC_CONST), np.float32)

    def put(name, a):
        a = np.asarray(a, np.float32)
        c[:a.shape[0], CONSTS[name][0]:CONSTS[name][0] + a.shape[1]] = a

    p = np.arange(P)
    put("ident", np.eye(P))
    causal = np.zeros((P, 512), np.float32)
    causal[:, 384:] = np.where(np.arange(P)[None] <= p[:, None], 0.0, NEG)
    put("causal", causal)
    inv = np.power(np.float32(THETA), -np.arange(0, ROT, 2, dtype=np.float32) / np.float32(ROT)).astype(np.float32)
    cos, sin = np.zeros((P, 5, ROT), np.float32), np.zeros((P, 5, ROT), np.float32)
    for i in range(5):
        pos = (i * P + p if i < NT else PAST + p % TQ).astype(np.float32)
        ang = pos[:, None] * inv[None]
        cos[:, i], sin[:, i] = np.tile(np.cos(ang), (1, 2)), np.tile(np.sin(ang), (1, 2))
    put("cos_tok", cos.reshape(P, -1))
    put("sin_tok", sin.reshape(P, -1))
    ang = (np.arange(NCS) * 16 + 31).astype(np.float32)[None] * inv[:, None]
    cb, sb = np.ones((DH, NCS), np.float32), np.zeros((DH, NCS), np.float32)
    cb[:8], cb[8:16], sb[:8], sb[8:16] = np.cos(ang), np.cos(ang), -np.sin(ang), np.sin(ang)
    put("cos_blk", np.tile(cb, (2, 1)))
    put("sin_blk", np.tile(sb, (2, 1)))
    blk = np.arange(NCP) * 16 + 31
    put("cmp_mask", np.concatenate([np.where(blk[None] <= (i * P + p)[:, None], 0.0, NEG) for i in range(NT)], 1))
    put("row_mask", (p >= 31)[:, None])
    row_b, row_h, row_t = p // 32, p % 32 // 4, p % 4
    tok = np.arange(TS)
    for q in range(NQ):
        b = q * QB + row_b
        a, o = CONSTS["pick_rows"][0] + q * P, CONSTS["new_mask"][0] + q * TS
        c[:TS, a:a + P] = tok[:, None] == (b * TQ + row_t)[None]
        ok = (tok[None] // TQ == b[:, None]) & (tok[None] % TQ <= row_t[:, None])
        c[:, o:o + TS] = np.where(ok, 0.0, NEG)
    put("pick_head", row_h[:, None] == np.arange(H)[None])
    put("win_mask", np.where(np.arange(TQ)[None] <= row_t[:, None], NEG, 0.0))
    cs, ss = np.arange(NCS)[:, None] * 16, np.arange(NSEL)[None] * 64
    put("overlap", np.clip(np.minimum(cs + 32, ss + 64) - np.maximum(cs, ss), 0, None) / 32.0)
    put("block_no", np.tile(np.arange(1, 15), (P, 1)))
    put("repeat4", np.arange(TQ)[:, None] == tok[None] % TQ)
    put("same_batch", tok[:, None] // TQ == tok[None] // TQ)
    put("group_mod", (p % 16)[:, None])
    return c


PARAMS = {}


def _params(items):
    at = 0
    for name, width in items:
        PARAMS[name] = (at, at + width)
        at += width
    return at


N_PARAM = _params([("norm_g", D), ("v_g", 512), ("v_b", 512), ("b_sp", 512), ("w2k", DH), ("w2kr", DH), ("w2v", DH),
                   ("b1k", 1), ("b1v", 1), ("b2k", 1), ("b2kr", 1), ("b2v", P)])


BETWEEN_ROWS = {0: (0, 1, 0, 1), 1: (0, 1, 0, 1), 3: (0, 1, 1, 1), 4: (0, 1, 1, 1)}
BEFORE_LAST_HIDDEN, AFTER_LAST_HIDDEN = 1, 1
AFTER_KEYS = [1, 1, 1, 1, 1, 1, 1, 1]
AFTER_STEP = [(1, 1, 1, 1, 1, 2),
              (1, 1, 1, 1, 1, 1)]
AFTER_FIRST_SCORES, AFTER_SCORES, BEFORE_LAST_PRODUCTS = 2, [1, 1, 1, 1, 3, 1, 1, 1, 1, 1, 1, 1, 1, 1, 2, 2], 3


def plan():
    order, groups = [], []
    for s, (name, kind, _, _) in enumerate(SLOTS):
        if kind in ("tm", "wo"):
            groups += [("main", s, i, 0) for i in (range(NT + 1) if kind == "tm" else LAST_TILES)]
        elif kind == "tr":
            groups += [("main", s, a, hf) for a in range(2) for hf in range(2)]
        else:
            groups += [("main", s, a, hf, y) for a in range(2) for hf in range(2) for y in range(2)]
    state = {"n": 0}

    def main(count):
        for _ in range(count):
            if state["n"] >= len(groups):
                return
            g = groups[state["n"]]
            order.append(g)
            state["n"] += 1
            if g[1] == SLOT["V1"] and g[2]:
                order.append(("ln", g[2] - 1))
                if g[2] == NT:
                    order.extend([("ln", NT), ("lnr",)])
            first = next(n for n, x in enumerate(groups) if x[1] == g[1])
            at = state["n"] - 1 - first
            if 1 <= g[1] < len(SLOTS) - 1:
                step = 2 if len(g) == 5 else 1
                if at in (step, 2 * step):
                    order.append(("low", g[1] + 1, at // step - 1))
                if at in (0, step):
                    order.append(("split", g[1] + 1, at // step))

    order += [("norm", 0), ("split", 0, 0), ("low", 0, 0), ("split", 0, 1), ("low", 0, 1), ("hT", 0), ("norm", 1)]
    for i in range(NT + 1):
        if i < NT:
            order += [("hT", i + 1)]
        if i + 2 <= NT:
            order += [("norm", i + 2)]
        main(1)
        order += {0: [("load_params",)], 1: [("split", 1, 0)], 2: [("low", 1, 0), ("split", 1, 1)], 3: [("low", 1, 1)]}.get(i, [])
    order += [("out_cmp",), ("wsT",)]
    main(5)
    order += [("rope", 0)]
    main(3)
    order += [("kT", 0)]
    main(2)
    order += [("rope", 1), ("gates",)]
    main(3)
    order += [("kT", 1), ("kTs",), ("wbd",)]
    main(3)
    order += [("gr",)]
    main(4)
    order += [("rope", 2)]
    main(3)
    order += [("qT", i) for i in range(NT)] + [("qTs",)]
    for c in range(6):
        for n in range(8 if c % 3 < 2 else 1):
            order += [("xt", c, n)]
            if n % 2:
                if c == 4 and n == 3:
                    order += [("sp", i) for i in range(NT + 1)]
                main(BETWEEN_ROWS[c][n // 2])
            if c and n == (1 if c % 3 < 2 else 0):
                order += [("kc", c - 1)]
        if c == 3:
            order += [("ln2", i) for i in range(NT + 1)]
        if c == 5:
            main(BEFORE_LAST_HIDDEN)
        order += [("hid", c)]
    main(AFTER_LAST_HIDDEN)
    order += [("kc", 5)]
    for q in range(NQ):
        for b in range(QB * q, QB * q + QB):
            order += [("qkT", b)]
            main(AFTER_KEYS[b])
            order += [("qkS", b)]
        for n, step in enumerate(("s_max", "s_turn", "s_imp", "s_mask", "s_exp", "s_scale")):
            if (q, step) == (NQ - 1, "s_scale"):
                order += [("cs", 0)]
            order += [(step, q)]
            main(AFTER_STEP[q][n])
        order += [("s_pv", q), ("s_out", q)]
    assert 59 <= state["n"] <= 61
    units = [(i, g, y) for i in range(NT) for g in range(G) for y in range(2)]
    limit = 35 + 8 + 16 + 16 + 10
    pending = []

    def products(keep):
        while len(pending) > keep:
            order.append(pending.pop(0))

    def turn_unit(u):
        for kt in range(units[u][0] + 1):
            order.append(("pt", u, kt))
            pending.append(("pp", u, kt))
            products(2)

    order += [("cx", 0)]
    for u, (i, g, y) in enumerate(units):
        n = u % 4
        order += [("ps", u)]
        if u:
            order += [("pn", u - 1)]
        else:
            main(AFTER_FIRST_SCORES)
            order += [("cn", 0)]
        main(min(AFTER_SCORES[u], limit - state["n"]))
        if n == 1:
            order += [("cv", i, 0), ("cv", i, 1)]
        if u:
            turn_unit(u - 1)
        if n == 0:
            order += [("ct", i, 0), ("ct", i, 1)]
        order += [("px", u)]
        if n == 0:
            products(0)
            order += [("oz", i - 1)] if i else []
        if i < NT - 1 and n:
            order += [(("cs", "cx", "cn")[n - 1], i + 1)]
    order += [("pn", len(units) - 1)]
    main(min(BEFORE_LAST_PRODUCTS, limit - state["n"]))
    turn_unit(len(units) - 1)
    products(0)
    order += [("oz", NT - 1)]
    for k in range(8):
        main(1 - k % 2)
        order += [("zs", k)]
    first_p = next(n for n, x in enumerate(groups) if SLOTS[x[1]][0] == "P0")
    main(first_p - state["n"])
    last = None
    while state["n"] < len(groups):
        s = groups[state["n"]]
        main(1)
        if last:
            order.append(last)
        last = None
        if len(s) == 5:
            if s[4]:
                last = ("mlo", 2 * (s[1] - SLOT["P0"]) + s[2], s[3])
            if s == ("main", SLOT["P3"], 1, 1, 1):
                order += [last, ("load_x",)]
                last = None
        elif s[1] == SLOT["WO3"]:
            last = ("fin", s[2])
    order.append(last)
    return order, units


ORDER, UNITS = plan()
MAIN = [s for s in ORDER if s[0] == "main"]
MAIN_AT = {s: n for n, s in enumerate(MAIN)}


def freed_by(s):
    if SLOTS[s[1]][1] in ("wp", "wo") or SLOTS[s[1]][0][0] == "Z":
        return "dve"
    return "act"


def t_uses(s):
    kind = s[0]
    if kind == "hT":
        return ["dve", "dve"]
    if kind in ("wsT", "wbd", "kT", "kTs", "qTs", "gr", "sp", "s_turn", "s_imp", "s_out", "cs"):
        return ["dve"]
    if kind == "qT":
        return ["act"]
    if kind == "xt":
        return ["act" if s[2] % 2 else "dve"]
    if kind == "qkT":
        return ["act", "dve", "act"]
    if kind == "s_pv":
        return ["dve", "act", "dve", "act"]
    if kind == "ct":
        return ["act" if s[2] else "dve"]
    if kind == "pt":
        return ["act" if (s[1] + s[2]) % 2 else "dve"]
    return []


T_USE, T_AT = [], {}
for _s in ORDER:
    T_AT[_s] = len(T_USE)
    T_USE += t_uses(_s)

RING = 3
LOADS = [(w, b) for w in ("kc", "vc") for b in list(range(NB)) + ["p"]] + \
        [(w, b) for b in range(NB) for w in ("ks", "kw")]
LOAD_AT = {x: n for n, x in enumerate(LOADS)}
PT_AT = {}
for _s in ORDER:
    if _s[0] in ("ct", "pt"):
        PT_AT[_s] = len(PT_AT)
NPT = 4


def part(c):
    return ("kc" if c < 3 else "vc"), c % 3


def load_freed(n):
    w, b = LOADS[n - RING]
    if w in ("ks", "kw"):
        return T_AT[("qkT", b)] + (2 if w == "ks" else 3)
    c = (0 if w == "kc" else 3) + (2 if b == "p" else b // QB)
    return T_AT[("xt", c, 0 if b == "p" else 2 * (b % QB) + 1)] + 1


def raw_count(r):
    two = lambda n: SLOTS[n // 2][0].startswith("ZA") or (SLOTS[n // 2][1] == "wp" and n % 2 == 0)
    return sum(32 if two(n) else 16 for n in range(r % NRAW, r + 1, NRAW))


def slot_used(sl):
    return max(n for n, x in enumerate(MAIN) if x[1] == sl) + 1


def hid_count(c):
    return [0, 2, 4, 5, 7, 9, 10][c]


FN_AT = {x: n for n, x in enumerate(x for x in MAIN if SLOTS[x[1]][0][0] in "UZ")}
ROPE_STEPS = [12, 24, 48]
N_OUT = 11


def nsa_gmlp_layer(nc, x_p, x_s, ck_cmp, cv_cmp, ck_sel, cv_sel, ck_win, cv_win, pages, w_in, w1k, w1v, w_sp,
                   w_pa, w_pb, w_o, final_g, params, consts, outs):
    (y_p, y_s, pk_cmp, pv_cmp, pk_sel, pv_sel, pk_win, pv_win,
     sk_cmp, sv_cmp, sk_sel, sv_sel, sk_win, sv_win, s_chunk) = outs
    ctx = ExitStack()
    with ctx:
        def sb(name, shape, dt=F32):
            return ctx.enter_context(nc.sbuf_tensor(name, shape, dt))

        def sem(name):
            return ctx.enter_context(nc.semaphore(name))

        h_hi, h_lo = sb("h_hi", [P, KD, T], F32R), sb("h_lo", [P, KD, T], F32R)
        w_hi, w_lo = sb("w_hi", [P, 2, KD, SW], F32R), sb("w_lo", [P, 2, KD, SW], F32R)
        raw = sb("raw", [P, NRAW, KD // 2, SW])
        sg = sb("sg", [P, 4, T])
        za = sb("za", [P, 4, T])
        cst = sb("cst", [P, NC_CONST])
        prm = sb("prm", [P, N_PARAM])
        wsT = sb("wsT", [P, 4, P])
        w_bd = sb("w_bd", [TS, 4, TS])
        kcT = sb("kcT", [P, NB, NCS])
        vc = sb("vc", [NCS, NB, P])
        kcp = sb("kcp", [P, G, NCP])
        vcp = sb("vcp", [NCP, P])
        gate = sb("gate", [P, NT + 1, 3 * H])
        gate_row = sb("gate_row", [P, NQ, 3])
        q_bd = sb("q_bd", [P, NB, G * J * TQ])
        k_newT = sb("k_newT", [P, 2, TS])
        o_row = sb("o_row", [P, P])
        tmp = sb("tmp", [P, 2, HALF])
        st = sb("st", [P, 128])
        pj_sum = sb("pj_sum", [NCS, 160])
        pick = sb("pick", [P, 14])
        penalty_sb = sb("penalty", [P, P])
        pages_sb = sb("pages_sb", [P, NB], I32)
        rows_sb = sb("rows_sb", [P, NB], U32)
        at0 = nc.sbuf_base
        arena = sb("arena", [P, 19200])

        def placed(name, col, shape, dt=F32):
            return nc.alloc_sbuf_tensor_at(name, shape, dt, offset=at0 + 4 * col)

        qT = placed("qT", 0, [P, J, TP])
        k_pad = placed("k_pad", 2048, [P, 2, G, TP])
        v_tok = placed("v_tok", 4096, [P, 2, NT + 1, P])
        U = placed("U", 5376, [P, 13824])
        x_hi, x_lo = placed("x_hi", 0, [P, 8, T], F32R), placed("x_lo", 4352, [P, 8, T], F32R)

        def cs(name, rows=P):
            return cst[0:rows, CONSTS[name][0]:CONSTS[name][1]]

        def pm(name, rows=P):
            return prm[0:rows, PARAMS[name][0]:PARAMS[name][1]]

        ident = cs("ident")
        penalty = penalty_sb[:, :]
        x_in = U[:, 0:5120].rearrange("p (i c) -> p i c", i=5)
        junk = U[:, 5120:6144]
        sg_flat = sg[:, :, :].rearrange("p g t -> p (g t)")
        xg = [sg_flat[:, 0:1024], sg_flat[:, 1024:2048], U[:, 6144:7168], U[:, 8192:9216], U[:, 9216:10240]]
        kq = U[:, 0:5120].rearrange("p (i c) -> p i c", i=5)
        vg = U[:, 5120:7680].rearrange("p (i c) -> p i c", i=5)
        ws_raw = U[:, 7680:8192].rearrange("p (g s) -> p g s", g=4)
        ring = U[:, 8192:11264].rearrange("p (r c) -> p r c", r=RING)
        w1_at = [U[:, 11264:13312].rearrange("p (j n) -> p j n", j=16), za[:, :, :].rearrange("p j t -> p (j t)")[:, 0:2048].rearrange("p (j n) -> p j n", j=16)]
        xt = U[:, 0:4096].rearrange("p (q g m) -> p q g m", q=4, g=G)
        xtp = U[:, 0:512].rearrange("p (q g m) -> p q g m", q=4, g=G)
        hid = U[:, 13312:13312 + 504].rearrange("p (g n) -> p g n", g=G)
        t1, t2 = U[:, 7680:7680 + 252], U[:, 7936:7936 + 252]
        rt = U[:, 13312:13824]
        vs = U[:, 0:4096].rearrange("p (b s d) -> p b s d", b=QB, s=8)
        vw = U[:, 4096:6144].rearrange("p (b s d) -> p b s d", b=QB, s=4)
        kt_s = U[:, 6144:7168]
        kt_w = U[:, 7168:7680]
        ptr = [U[:, 7680:8192], U[:, 12928:13440]]
        pts = U[:, 13440:13824]
        ps = U[:, 11264:12928]
        SEL, WIN, CMP = 0, 1056, 1600
        pb = U[:, 0:4096].rearrange("p (b j k) -> p b j k", b=2, j=J)
        ptb = U[:, 4096:6144].rearrange("p (r n) -> p r n", r=NPT)
        cp = U[:, 6144:6144 + J * G * NCP]
        sig = U[:, 5120:13824].rearrange("p (n t) -> p n t", t=T)

        def sig_at(b, d):
            n = 3 + 8 * b + d
            return sig[:, n if n < 16 else n - 16, :]

        xr_slots = U[:, 0:5120].rearrange("p (i c) -> p i c", i=5)
        xr = [xr_slots[:, (i + 4) % 5, :] for i in range(NT + 1)]

        bank = [ctx.enter_context(nc.psum_tensor(n, [P, 512], F32)) for n in ("m0", "m1", "t0", "t1", "s0", "s1", "s2", "o")]
        M, TB, S, O = bank[0:2], bank[2:4], bank[4:7], bank[7]

        x_loaded = [sem(f"x_loaded{n}") for n in range(NT + 1)]
        xg_ready = sem("xg_ready")
        norm_g_loaded, ident_loaded, const_loaded, small_loaded = (sem("norm_g_loaded"), sem("ident_loaded"),
                                                                   sem("const_loaded"), sem("small_loaded"))
        raw_loaded = [sem(f"raw_loaded{n}") for n in range(NRAW)]
        w1_loaded = [sem("w1k_loaded"), sem("w1v_loaded")]
        ring_loaded = [sem(f"ring_loaded{n}") for n in range(RING)]
        v_loaded = sem("v_loaded")
        xr_loaded = [sem(f"xr_loaded{n}") for n in range(NT + 1)]
        x_split, x_lo_done, fg_loaded = sem("x_split"), sem("x_lo_done"), sem("fg_loaded")
        out_done, cmp_out = sem("out_done"), sem("cmp_out")
        win_out, y_out = sem("win_out"), sem("y_out")
        rows_ready, ws_masked, rope_step = sem("rows_ready"), sem("ws_masked"), sem("rope_step")
        pads_zero, st_ready, mix_fn, pv_part, pt_used = (sem("pads_zero"), sem("st_ready"), sem("mix_fn"), sem("pv_part"),
                                                         sem("pt_used"))
        ssq_ready, root_in, root_done, h_ready = sem("ssq_ready"), sem("root_in"), sem("root_done"), sem("h_ready")
        hi_done, lo_done = sem("hi_done"), sem("lo_done")
        hT_hi = sem("hT_hi")
        main_done, main_act, main_dve = sem("main_done"), sem("main_act"), sem("main_dve")
        t_done, t_act, t_dve = sem("t_done"), sem("t_act"), sem("t_dve")
        gl_tanh, gate_ready = sem("gl_tanh"), sem("gate_ready")
        var_ready, std_ready, vn_ready = sem("var_ready"), sem("std_ready"), sem("vn_ready")
        hid_sum, hid_ready, kc_done, kc_ready = sem("hid_sum"), sem("hid_ready"), sem("kc_done"), sem("kc_ready")
        act_fn = sem("act_fn")
        qk_done = sem("qk_done")
        s_bias, s_cexp, s_cp, s_pj, s_bias2, s_exp, s_p = (sem("s_bias"), sem("s_cexp"), sem("s_cp"), sem("s_pj"),
                                                           sem("s_bias2"), sem("s_exp"), sem("s_p"))
        o_done, o_row_ready = sem("o_done"), sem("o_row_ready")
        c_in, c_exp, c_p = sem("c_in"), sem("c_exp"), sem("c_p")
        p_scored, p_bias, p_masked, p_exp, p_scaled = (sem("p_scored"), sem("p_bias"), sem("p_masked"), sem("p_exp"),
                                                       sem("p_scaled"))
        mix_ready = sem("mix_ready")
        m_sum, m_hi, m_lo = sem("m_sum"), sem("m_hi"), sem("m_lo")
        f_scaled, f_out_pool = sem("f_scaled"), sem("f_out_pool")
        f_ssq, f_ms, f_root, f_out = sem("f_ssq"), sem("f_ms"), sem("f_root"), sem("f_out")
        dve_step = sem("dve_step")

        def count(which, upto, engine):
            return sum(1 for e in which[:upto] if e == engine)

        main_by = [freed_by(s) for s in MAIN]

        def wait_main_bank(eng, n):
            if n >= 2:
                e = main_by[n - 2]
                eng.wait_ge(main_act if e == "act" else main_dve, count(main_by, n - 1, e))

        def wait_t_bank(eng, t):
            if t >= 2:
                e = T_USE[t - 2]
                eng.wait_ge(t_act if e == "act" else t_dve, count(T_USE, t - 1, e))

        def wait_evacuated(eng, t):
            e = T_USE[t]
            eng.wait_ge(t_act if e == "act" else t_dve, count(T_USE, t + 1, e))

        def wait_main_read(eng, s):
            n = MAIN_AT[s]
            e = main_by[n]
            eng.wait_ge(main_act if e == "act" else main_dve, count(main_by, n + 1, e))

        def wait_tmp_read(eng, k):
            s = list(FN_AT)[k]
            if SLOTS[s[1]][0].startswith("ZA"):
                wait_main_read(eng, s)
            else:
                eng.wait_ge(mix_fn, k + 1 - (8 if k >= 16 else 0))

        def tok(i):
            return slice(i * P, (i + 1) * P) if i < NT else slice(TP, T)

        def n_sp(i):
            return P if i < NT else TS

        def split_parts(sl, hf, r, w):
            ks = slice(4 * hf, 4 * hf + 4)
            hi, lo, x = w_hi[:, sl % 2, ks, 0:w], w_lo[:, sl % 2, ks, 0:w], raw[:, r, :, 0:w]
            if not SLOTS[sl][0].startswith("ZA"):
                return [(hi, lo, x)]
            xs = x.rearrange("p k (g j d) -> p k g j d", g=G, j=2)
            return [(*(a[:, :, j * P:(j + 1) * P].rearrange("p k (g d) -> p k g d", g=G) for a in (hi, lo)), xs[:, :, :, j, :])
                    for j in range(2)]

        def xt_parts(c, n, tb):
            if c % 3 == 2:
                return [(xtp[64 * r:64 * r + 64, :, g, :], tb[64 * g:64 * g + 64, 256 * r:256 * r + 256].rearrange("p (q m) -> p q m", q=4))
                        for r in range(2) for g in range(G)]
            b, r = divmod(n, 2)
            return [(xt[64 * r:64 * r + 64, :, g, b * P:(b + 1) * P], tb[64 * g:64 * g + 64, :].rearrange("p (q m) -> p q m", q=4))
                    for g in range(G)]

        def last_of(name):
            return ("main", SLOT[name], NT, 0)

        w_dram = w_in.rearrange("(k p) n -> p k n", p=P)
        wo_dram = w_o.rearrange("(k p) n -> p k n", p=P)

        block = ctx.enter_context(nc.Block())

        @block.sync
        def _(sp):
            def load_raw(r):
                s, hf = divmod(r, 2)
                if s >= len(SLOTS):
                    return
                name, kind, c0, w = SLOTS[s]
                if r >= NRAW:
                    sp.wait_ge(lo_done, r - NRAW + 1)
                dst = raw[:, r % NRAW, :, 0:w]
                ks = slice(4 * hf, 4 * hf + 4)
                if name.startswith("ZA"):
                    n = int(name[2])
                    for g in range(G):
                        a = c0 + g * 256 + n * 128
                        sp.dma_start(raw[:, r % NRAW, :, g * 128:g * 128 + 128],
                                     w_dram[:, ks, a:a + 128]).then_inc(raw_loaded[r % NRAW], 16)
                elif kind == "wp" and hf == 0:
                    for g in range(G):
                        sp.dma_start(raw[64 * g:64 * g + 64, r % NRAW, :, 0:w],
                                     w_pa.rearrange("(g k d) n -> g d k n", g=G, k=J)[g, :, :, c0:c0 + w]).then_inc(raw_loaded[r % NRAW], 16)
                elif kind == "wp":
                    sp.dma_start(dst, w_pb.rearrange("(k p) n -> p k n", p=P)[:, :, c0:c0 + w]).then_inc(raw_loaded[r % NRAW], 16)
                elif kind == "wo":
                    sp.dma_start(dst, wo_dram[:, ks, c0:c0 + w]).then_inc(raw_loaded[r % NRAW], 16)
                else:
                    sp.dma_start(dst, w_dram[:, ks, c0:c0 + w]).then_inc(raw_loaded[r % NRAW], 16)

            def load_x(i):
                sp.dma_start(x_in[0:n_sp(i), i, :], x_p[tok(i), :] if i < NT else x_s).then_inc(x_loaded[i], 16)

            load_x(0)
            sp.dma_start(pm("norm_g"), params[:, 0:D]).then_inc(norm_g_loaded, 16)
            sp.dma_start(ident, consts[:, 0:P]).then_inc(ident_loaded, 16)
            load_raw(0)
            load_raw(1)
            load_x(1)
            load_x(2)
            load_x(3)
            load_raw(2)
            load_x(4)
            n_win = 0
            for s in ORDER:
                if s[0] == "low":
                    load_raw(2 * s[1] + s[2] + NRAW)
                elif s[0] == "load_params":
                    sp.dma_start(prm[:, D:N_PARAM], params[:, D:N_PARAM]).then_inc(const_loaded, 16)
                    sp.dma_start(cst[:, P:NC_CONST], consts[:, P:NC_CONST]).then_inc(const_loaded, 16)
                    sp.dma_start(pages_sb[:, :], pages).then_inc(small_loaded, 16)
                    sp.dma_start(ws_raw, w_sp).then_inc(small_loaded, 16)
                    sp.dma_start(w1_at[0], w1k.rearrange("(j p) n -> p j n", p=P)).then_inc(w1_loaded[0], 16)
                    sp.dma_start(w1_at[1], w1v.rearrange("(j p) n -> p j n", p=P)).then_inc(w1_loaded[1], 16)
                elif s[0] == "xt" and s[2] == 0 and s[1] % 3 < 2:
                    for b in range(2 * n_win, 2 * n_win + 2):
                        sp.dma_start(sk_win[b, 0:512 - TQ, :], ck_win[b, TQ:512, :]).then_inc(win_out, 16)
                        sp.dma_start(sv_win[b, 0:512 - TQ, :], cv_win[b, TQ:512, :]).then_inc(win_out, 16)
                    n_win += 1
                elif s[0] == "oz" and s[1] == NT - 1:
                    sp.wait_ge(pt_used, len(PT_AT))
                    sp.dma_start(xr[0][:, :], x_p[tok(0), :]).then_inc(xr_loaded[0], 16)
                    sp.dma_start(pm("norm_g"), final_g).then_inc(fg_loaded, 16)
                elif s[0] == "load_x":
                    sp.wait_ge(main_done, MAIN_AT[("main", SLOT["P3"], 1, 1, 1)] + 1)
                    for i in range(1, NT):
                        sp.dma_start(xr[i][:, :], x_p[tok(i), :]).then_inc(xr_loaded[i], 16)
                    sp.dma_start(xr[NT][96:128, :], x_s).then_inc(xr_loaded[NT], 16)
                elif s[0] == "fin":
                    i = s[1]
                    for n in range(2):
                        k = LAST_TILES.index(i)
                        if n and k < NT:
                            sp.wait_ge(f_out_pool, k + 1)
                        else:
                            sp.wait_ge(f_out, k + 1 + n)
                        c = (slice(0, FIN_CUT), slice(FIN_CUT, D))[n]
                        if i < NT:
                            sp.dma_start(y_p[tok(i), c], xr[i][:, c]).then_inc(y_out, 16)
                        else:
                            sp.dma_start(y_s[:, c], xr[NT][96:128, c]).then_inc(y_out, 16)
            sp.wait_ge(y_out, 16 * 10)
            sp.wait_ge(win_out, 16 * 2 * NB)
            sp.wait_ge(out_done, 16 * N_OUT)
            sp.wait_ge(cmp_out, 32)

        @block.gpsimd
        def _(pool):
            pool.wait_ge(norm_g_loaded, 16)
            for i in range(NT + 1):
                pool.wait_ge(x_loaded[i], 16)
                pool.tensor_tensor(xg[i][0:n_sp(i), :], x_in[0:n_sp(i), i, :], pm("norm_g", n_sp(i)), ALU.mult).then_inc(xg_ready, 1)
            pool.memset(k_pad[:, :, :, :], 0.0).then_inc(pads_zero, 1)
            pool.memset(q_bd[:, :, :], 0.0).then_inc(pads_zero, 1)
            pool.memset(kcp[:, :, :], 0.0).then_inc(pads_zero, 1)
            pool.memset(st[:, 64:80], 0.0).then_inc(pads_zero, 1)
            pool.wait_ge(small_loaded, 32)
            pool.affine_select(out=ws_raw, in_=ws_raw, compare_op=ALU.is_ge, fill=0.0, base=0,
                               pattern=[[0, 4], [-1, P]], channel_multiplier=1).then_inc(ws_masked, 1)
            steps = [0]

            def rope(x, cos, sin, a, b):
                pool.tensor_tensor(a, x, cos, ALU.mult).then_inc(rope_step, 1)
                pool.tensor_tensor(b, x, sin, ALU.mult).then_inc(rope_step, 1)
                steps[0] += 2
                pool.wait_ge(rope_step, steps[0])
                nd = len(a.shape)
                lo, hi = (slice(None),) * (nd - 1) + (slice(0, 8),), (slice(None),) * (nd - 1) + (slice(8, 16),)
                pool.tensor_tensor(x[lo], a[lo], b[hi], ALU.subtract).then_inc(rope_step, 1)
                pool.tensor_tensor(x[hi], a[hi], b[lo], ALU.add).then_inc(rope_step, 1)
                steps[0] += 2
                pool.wait_ge(rope_step, steps[0])

            def rope_all(c0, heads):
                cos = cs("cos_tok").rearrange("p (i r) -> p i r", i=5)
                sin = cs("sin_tok").rearrange("p (i r) -> p i r", i=5)
                for rows, i0, i1 in [(P, 0, 2), (P, 2, 4), (TS, NT, NT + 1)]:
                    n = i1 - i0
                    for h0 in range(0, heads, 4):
                        hn = min(4, heads - h0)
                        a, b = (rt[0:rows, o:o + n * hn * ROT].rearrange("p (i h r) -> p i h r", i=n, h=hn) for o in (0, 256))
                        x = kq[0:rows, i0:i1, c0 + h0 * DH:c0 + (h0 + hn) * DH].rearrange("p i (h d) -> p i h d", h=hn)[:, :, :, 0:ROT]
                        shape = [rows, n, hn, ROT]
                        rope(x, cos[0:rows, i0:i1, :].unsqueeze(2).broadcast_to(shape),
                             sin[0:rows, i0:i1, :].unsqueeze(2).broadcast_to(shape), a, b)

            def store(dst_p, dst_s, src_p, src_s, done):
                pool.dma_start(dst_p.rearrange("(i p) c -> p i c", p=P), src_p).then_inc(done, 16)
                pool.dma_start(dst_s, src_s).then_inc(out_done, 16)

            def load(n):
                w, b = LOADS[n]
                if n >= RING:
                    pool.wait_ge(t_done, load_freed(n))
                if (w, b) == ("kc", "p"):
                    pool.wait_ge(cmp_out, 32)
                slot, done = ring[:, n % RING, :], ring_loaded[n % RING]
                if b == "p":
                    src = pk_cmp if w == "kc" else pv_cmp
                    pool.dma_start(ring[0:64, n % RING, :], src.rearrange("(m r) c -> m (r c)", r=8)).then_inc(done, 16)
                elif w == "kw":
                    pool.dma_start(ring[:, n % RING, 0:512], ck_win[b].rearrange("(m r) c -> m (r c)", r=4)).then_inc(done, 16)
                else:
                    src = {"kc": ck_cmp, "vc": cv_cmp, "ks": ck_sel}[w]
                    pool.indirect_dma_start(slot, None, src, bass.IndirectOffsetOnAxis(rows_sb[:, b:b + 1], 0)).then_inc(done, 16)

            loaded = [0]

            def load_upto(n):
                while loaded[0] < min(n, len(LOADS)):
                    load(loaded[0])
                    loaded[0] += 1

            new_rows = lambda d: d[:, 512 - TQ:512, :]
            for s in ORDER:
                if s == ("out_cmp",):
                    wait_main_read(pool, last_of("B0"))
                    store(pk_cmp, sk_cmp, kq[:, 0:NT, 256:384], kq[0:TS, NT, 256:384], cmp_out)
                    store(pv_cmp, sv_cmp, kq[:, 0:NT, 384:512], kq[0:TS, NT, 384:512], cmp_out)
                    pool.wait_ge(rows_ready, 1)
                    load_upto(RING)
                elif s[0] == "rope":
                    if s[1] < 2:
                        wait_main_read(pool, last_of("B1" if s[1] == 0 else "C0"))
                        rope_all(128 * s[1], G)
                        c0 = 128 * s[1]
                        if s[1] == 0:
                            store(pk_sel, sk_sel, kq[:, 0:NT, c0:c0 + 128], kq[0:TS, NT, c0:c0 + 128], out_done)
                            store(pv_sel, sv_sel, v_tok[:, 0, 0:NT, :], v_tok[0:TS, 0, NT, :], out_done)
                        else:
                            store(pk_win, new_rows(sk_win), kq[:, 0:NT, c0:c0 + 128], kq[0:TS, NT, c0:c0 + 128], out_done)
                            store(pv_win, new_rows(sv_win), v_tok[:, 1, 0:NT, :], v_tok[0:TS, 1, NT, :], out_done)
                    else:
                        wait_main_read(pool, last_of("A1"))
                        rope_all(512, H)
                elif s == ("ln2", NT):
                    pool.wait_ge(vn_ready, NT + 1)
                    pool.dma_start(s_chunk, vg[0:TS, NT, :]).then_inc(out_done, 16)
                elif s[0] == "xt" and s[2] % 2 == 0:
                    w, c = part(s[1])
                    load_upto(LOAD_AT[(w, "p" if c == 2 else c * QB + s[2] // 2)] + RING + 1)
                elif s[0] == "qkT":
                    b = s[1]
                    load_upto(LOAD_AT[("ks", b)] + RING + 1)
                    if b == 0:
                        pool.wait_ge(hid_sum, 10)
                        pool.wait_ge(kc_done, 6)
                        pool.wait_ge(kc_ready, 6)
                    elif b == QB:
                        pool.wait_ge(o_done, 1)
                    n = b % QB
                    pool.indirect_dma_start(U[:, n * 1024:n * 1024 + 1024], None, cv_sel,
                                            bass.IndirectOffsetOnAxis(rows_sb[:, b:b + 1], 0)).then_inc(v_loaded, 16)
                    pool.dma_start(U[:, 4096 + n * 512:4608 + n * 512], cv_win[b].rearrange("(m r) c -> m (r c)", r=4)).then_inc(v_loaded, 16)

                elif s[0] == "fin" and s[1] != LAST_TILES[-1]:
                    i, c = s[1], slice(FIN_CUT, D)
                    k = LAST_TILES.index(i)
                    pool.wait_ge(f_out, k + 1)
                    if k == 0:
                        pool.wait_ge(fg_loaded, 16)
                    pool.tensor_scalar(xr[i][:, c], xr[i][:, c], st[:, 10 + i:11 + i], None, ALU.mult).then_inc(f_scaled, 1)
                    pool.wait_ge(f_scaled, k + 1)
                    pool.tensor_tensor(xr[i][:, c], xr[i][:, c], pm("norm_g")[:, c], ALU.mult).then_inc(f_out_pool, 1)

        @block.scalar
        def _(act):
            for s in ORDER:
                kind = s[0]
                t = T_AT[s]
                if kind == "norm":
                    i = s[1]
                    r = n_sp(i)
                    if i == 0:
                        act.wait_ge(st_ready, 1)
                        nc.scalar.activation(st[:, 29:30], st[:, 29:30], ACT.Sqrt)
                    act.wait_ge(x_loaded[i], 16)
                    if i:
                        act.wait_ge(ssq_ready, i)
                    nc.scalar.activation(junk[0:r, :], x_in[0:r, i, :], ACT.Square,
                                         accum_out=st[0:r, i:i + 1]).then_inc(ssq_ready, 1)
                    act.wait_ge(root_in, i + 1)
                    nc.scalar.activation(st[0:r, 10 + i:11 + i], st[0:r, 5 + i:6 + i], ACT.Sqrt).then_inc(root_done, 1)
                elif kind == "split":
                    _, sl, hf = s
                    r, w = 2 * sl + hf, SLOTS[sl][3]
                    act.wait_ge(raw_loaded[r % NRAW], raw_count(r))
                    if sl >= 2:
                        act.wait_ge(main_done, slot_used(sl - 2))
                    for hi, lo, x in split_parts(sl, hf, r % NRAW, w):
                        ins = nc.scalar.copy(hi, x)
                    ins.then_inc(hi_done, 1)
                elif kind == "hT":
                    i = s[1]
                    n = n_sp(i)
                    for hf in range(2):
                        act.wait_ge(t_done, t + hf + 1)
                        nc.scalar.copy(h_hi[:, 4 * hf:4 * hf + 4, tok(i)],
                                       TB[(t + hf) % 2][:, 0:4 * n].rearrange("p (k n) -> p k n", k=4)).then_inc(hT_hi, 1)
                elif kind == "main" and SLOTS[s[1]][1] != "wp":
                    name, mk = SLOTS[s[1]][0], SLOTS[s[1]][1]
                    n = MAIN_AT[s]
                    if mk == "wo":
                        i = s[2]
                        r = slice(0, P) if i < NT else slice(96, 128)
                        c, k = s[1] - SLOT["WO0"], n - MAIN_AT[("main", SLOT["WO0"], LAST_TILES[0], 0)]
                        wait_main_read(act, s)
                        if k:
                            act.wait_ge(f_ssq, k)
                        else:
                            act.wait_ge(m_lo, 16)
                        nc.scalar.activation(U[r, 5120:5376], xr[i][r, 256 * c:256 * c + 256], ACT.Square,
                                             accum_out=st[r, 20 + 4 * i + c:21 + 4 * i + c]).then_inc(f_ssq, 1)
                        continue
                    act.wait_ge(main_done, n + 1)
                    m = M[n % 2]
                    if mk == "tm":
                        i = s[2]
                        r = n_sp(i)
                        src = m[0:P, :] if i < NT else m[96:128, :]
                        if name == "B0":
                            nc.scalar.copy(kq[0:r, i, 256:512], src[:, 0:256]).then_inc(main_act, 1)
                        elif name == "B1":
                            nc.scalar.copy(kq[0:r, i, 0:128], src[:, 0:128])
                            nc.scalar.copy(v_tok[0:r, 0, i, :], src[:, 128:256]).then_inc(main_act, 1)
                        elif name == "C0":
                            nc.scalar.copy(kq[0:r, i, 128:256], src[:, 0:128])
                            nc.scalar.copy(v_tok[0:r, 1, i, :], src[:, 128:256])
                            nc.scalar.copy(gate[0:r, i, :], src[:, 256:280]).then_inc(main_act, 1)
                        elif name[0] == "A":
                            g = int(name[1])
                            nc.scalar.copy(kq[0:r, i, 512:1024].rearrange("p (j g d) -> p j g d", j=J, g=G)[:, :, g, :],
                                           src[:, 0:256].rearrange("p (j d) -> p j d", j=J)).then_inc(main_act, 1)
                        else:
                            c0 = 256 * int(name[1])
                            nc.scalar.activation(vg[0:r, i, c0:c0 + 256], src[:, 0:256], ACT.Gelu_apprx_tanh)\
                                .then_inc(main_act, 1)
                    elif name[0] == "U":
                        k = FN_AT[s]
                        if k >= 2:
                            act.wait_ge(mix_fn, k - 1)
                        nc.scalar.activation(tmp[:, k % 2, :], m[:, 0:HALF], ACT.Gelu_apprx_tanh).then_inc(main_act, 1)
                    elif name[0] == "Z":
                        k = FN_AT[s]
                        wait_tmp_read(act, k - 2)
                        nc.scalar.activation(tmp[:, k % 2, :], m[:, 0:HALF], ACT.Tanh, scale=0.5).then_inc(act_fn, 1)
                    else:
                        d = 2 * int(name[2]) + s[2]
                        nc.scalar.activation(sig_at(int(name[1] == "B"), d)[:, s[3] * HALF:(s[3] + 1) * HALF], m[:, 0:HALF],
                                             ACT.Tanh, scale=0.5).then_inc(main_act, 1)
                elif kind == "gates":
                    wait_main_read(act, last_of("C0"))
                    nc.scalar.activation(gate[:, 0:NT, :], gate[:, 0:NT, :], ACT.Tanh, scale=0.5)
                    nc.scalar.activation(gate[0:TS, NT, :], gate[0:TS, NT, :], ACT.Tanh, scale=0.5).then_inc(gl_tanh, 1)
                elif kind == "qT":
                    i = s[1]
                    act.wait_ge(t_done, t + 1)
                    nc.scalar.copy(qT[:, :, tok(i)], TB[t % 2][:, :].rearrange("p (j n) -> p j n", j=J)).then_inc(t_act, 1)
                elif kind == "lnr":
                    act.wait_ge(var_ready, NT + 1)
                    nc.scalar.activation(st[:, 25:30], st[:, 20:25], ACT.Sqrt).then_inc(std_ready, 1)
                elif kind == "xt" and T_USE[t] == "act":
                    c, n = s[1], s[2]
                    act.wait_ge(t_done, t + 1)
                    if n == 1 and c:
                        act.wait_ge(hid_sum, hid_count(c))
                    if n == 1 and c == 0:
                        act.wait_ge(out_done, 16 * (N_OUT - 1))
                        act.wait_ge(cmp_out, 32)
                    for dst, src in xt_parts(c, n, TB[t % 2]):
                        ins = nc.scalar.copy(dst, src)
                    ins.then_inc(t_act, 1)
                elif kind == "hid":
                    c = s[1]
                    b1 = pm("b1k" if c < 3 else "b1v")
                    if c:
                        act.wait_ge(kc_done, c)
                    else:
                        act.wait_ge(rope_step, ROPE_STEPS[2])
                    if c % 3 < 2:
                        for g in range(G):
                            act.wait_ge(hid_sum, hid_count(c) + g + 1)
                            nc.scalar.activation(hid[:, g, :], S[g][:, 0:252], ACT.Gelu_apprx_tanh, bias=b1).then_inc(hid_ready, 1)
                    else:
                        act.wait_ge(hid_sum, hid_count(c) + 1)
                        nc.scalar.activation(hid[:, 0, 0:2 * NCP], S[0][:, 0:2 * NCP], ACT.Gelu_apprx_tanh, bias=b1).then_inc(hid_ready, 1)
                elif kind == "qkT":
                    b = s[1]
                    for k, dst in ((0, kt_s[:, 0:512]), (2, kt_w)):
                        act.wait_ge(t_done, t + k + 1)
                        if b:
                            act.wait_ge(qk_done, b)
                        else:
                            act.wait_ge(out_done, 16 * N_OUT)
                        nc.scalar.copy(dst, TB[(t + k) % 2][:, :]).then_inc(t_act, 1)
                elif kind == "s_max":
                    q = s[1]
                    act.wait_ge(s_bias, q + 1)
                    nc.scalar.activation(ps[:, CMP:CMP + NCS], O[:, 0:NCS], ACT.Exp, bias=st[:, 31:32], scale=SCALE,
                                         accum_out=st[:, 32:33]).then_inc(s_cexp, 1)
                elif kind == "s_exp":
                    q = s[1]
                    act.wait_ge(s_bias2, q + 1)
                    nc.scalar.activation(ps[:, 0:1056], ps[:, 0:1056], ACT.Exp, bias=st[:, 46:47], scale=SCALE,
                                         accum_out=st[:, 48:49])
                    nc.scalar.activation(ps[:, WIN:WIN + 512], S[2][:, :], ACT.Exp, bias=st[:, 47:48], scale=SCALE,
                                         accum_out=st[:, 49:50])
                    nc.scalar.activation(ps[:, WIN + 512:WIN + 544], ps[:, WIN + 512:WIN + 544], ACT.Exp, bias=st[:, 47:48],
                                         scale=SCALE, accum_out=st[:, 50:51]).then_inc(s_exp, 1)
                elif kind == "s_pv":
                    for k in (1, 3):
                        act.wait_ge(t_done, t + k + 1)
                        dst = ptr[1]
                        if k == 3:
                            act.wait_ge(pv_part, 2 * s[1] + 1)
                        nc.scalar.copy(dst, TB[(t + k) % 2][:, :]).then_inc(t_act, 1)
                elif kind == "cx":
                    act.wait_ge(c_in, s[1] + 1)
                    nc.scalar.activation(cp, cp, ACT.Exp, scale=SCALE).then_inc(c_exp, 1)
                elif kind in ("ct", "pt") and T_AT[s] < len(T_USE) and t_uses(s) == ["act"]:
                    act.wait_ge(t_done, t + 1)
                    r = PT_AT[s]
                    if r >= NPT:
                        act.wait_ge(pt_used, r - NPT + 1)
                    rows = NCP if kind == "ct" else P
                    nc.scalar.copy(ptb[0:rows, r % NPT, :], TB[t % 2][0:rows, :]).then_inc(t_act, 1)
                elif kind == "px":
                    u = s[1]
                    n = (UNITS[u][0] + 1) * P
                    act.wait_ge(p_bias, u + 1)
                    m = 80 + 20 * (u % 2)
                    for j in range(J):
                        ins = nc.scalar.activation(pb[:, u % 2, j, 0:n], pb[:, u % 2, j, 0:n], ACT.Exp, bias=st[:, m + 4 + j:m + 5 + j],
                                                   scale=SCALE, accum_out=st[:, m + 8 + j:m + 9 + j])
                    ins.then_inc(p_exp, 1)
                elif kind == "zs":
                    k = s[1]
                    if k == 0:
                        act.wait_ge(pt_used, len(PT_AT))
                        act.wait_ge(mix_ready, NT)
                    if k == 4:
                        act.wait_ge(mix_fn, 16)
                    nc.scalar.copy(x_hi[:, k, :], (za if k < 4 else sg)[:, k % 4, :]).then_inc(x_split, 1)
                elif kind == "main" and s[4]:
                    dt, hf = 2 * (s[1] - SLOT["P0"]) + s[2], s[3]
                    act.wait_ge(m_sum, 2 * dt + hf + 1)
                    c = slice(hf * HALF, (hf + 1) * HALF)
                    nc.scalar.copy(h_hi[:, dt, c], sig_at(0, dt)[:, c]).then_inc(m_hi, 1)
                elif kind == "fin":
                    i = s[1]
                    r = slice(0, P) if i < NT else slice(96, 128)
                    act.wait_ge(f_ms, LAST_TILES.index(i) + 1)
                    nc.scalar.activation(st[r, 10 + i:11 + i], st[r, 5 + i:6 + i], ACT.Sqrt).then_inc(f_root, 1)

        @block.vector
        def _(dve):
            v = nc.vector
            steps = [0]

            def seq(ins):
                steps[0] += 1
                ins.then_inc(dve_step, 1)
                dve.wait_ge(dve_step, steps[0])

            def inverse_root(root, x, a):
                seq(v.reciprocal(root, root))
                if x.shape[1] == 1:
                    seq(v.scalar_tensor_tensor(a, root, x, root, ALU.mult, ALU.mult))
                else:
                    seq(v.tensor_tensor(a, root, root, ALU.mult))
                    seq(v.tensor_tensor(a, a, x, ALU.mult))
                seq(v.tensor_scalar(a, a, -0.5, 1.5, ALU.mult, ALU.add))
                seq(v.tensor_tensor(root, root, a, ALU.mult))

            for s in ORDER:
                kind = s[0]
                t = T_AT[s]
                if kind == "norm":
                    i = s[1]
                    r = n_sp(i)
                    if i == 0:
                        v.memset(st[:, 0:30], 1.0).then_inc(st_ready, 1)
                    dve.wait_ge(ssq_ready, i + 1)
                    v.tensor_scalar(st[0:r, 5 + i:6 + i], st[0:r, i:i + 1], 1.0 / D, EPS, ALU.mult, ALU.add).then_inc(root_in, 1)
                    dve.wait_ge(root_done, i + 1)
                    inverse_root(st[0:r, 10 + i:11 + i], st[0:r, 5 + i:6 + i], st[0:r, 120:121])
                    dve.wait_ge(xg_ready, i + 1)
                    v.tensor_scalar(xg[i][0:r, :], xg[i][0:r, :], st[0:r, 10 + i:11 + i], None, ALU.mult).then_inc(h_ready, 1)
                elif kind == "out_cmp":
                    dve.wait_ge(small_loaded, 32)
                    dve.wait_ge(const_loaded, 32)
                    v.tensor_scalar(rows_sb[:, :], pages_sb[:, :], 16.0, cs("group_mod"), ALU.mult, ALU.add).then_inc(rows_ready, 1)
                elif kind == "low":
                    _, sl, hf = s
                    r, w = 2 * sl + hf, SLOTS[sl][3]
                    dve.wait_ge(hi_done, r + 1)
                    for hi, lo, x in split_parts(sl, hf, r % NRAW, w):
                        ins = v.tensor_tensor(lo, x, hi.bitcast(F32), ALU.subtract)
                    ins.then_inc(lo_done, 1)
                elif kind == "hT":
                    i = s[1]
                    n = n_sp(i)
                    for hf in range(2):
                        dve.wait_ge(hT_hi, 2 * i + hf + 1)
                        v.tensor_tensor(h_lo[:, 4 * hf:4 * hf + 4, tok(i)],
                                        TB[(t + hf) % 2][:, 0:4 * n].rearrange("p (k n) -> p k n", k=4),
                                        h_hi[:, 4 * hf:4 * hf + 4, tok(i)].bitcast(F32), ALU.subtract).then_inc(t_dve, 1)
                elif kind == "wsT":
                    dve.wait_ge(t_done, t + 1)
                    v.tensor_copy(wsT[:, :, :], TB[t % 2][:, :].rearrange("p (g n) -> p g n", g=4)).then_inc(t_dve, 1)
                elif kind == "wbd":
                    dve.wait_ge(t_done, t + 1)
                    same = cs("same_batch", TS).rearrange("p (b t) -> p b t", b=NB)
                    for g in range(4):
                        ins = v.tensor_tensor(w_bd[:, g, :].rearrange("p (b t) -> p b t", b=NB),
                                              TB[t % 2][0:TS, 4 * g:4 * g + 4].unsqueeze(1).broadcast_to([TS, NB, TQ]), same, ALU.mult)
                    ins.then_inc(t_dve, 1)
                elif kind == "kT":
                    y = s[1]
                    dve.wait_ge(pads_zero, 4)
                    dve.wait_ge(t_done, t + 1)
                    for g in range(G):
                        ins = v.tensor_copy(k_pad[64 * g:64 * g + 64, y, g, :], TB[t % 2][64 * g:64 * g + 64, :])
                    ins.then_inc(t_dve, 1)
                elif kind == "kTs":
                    dve.wait_ge(t_done, t + 1)
                    v.tensor_copy(k_newT[:, :, :], TB[t % 2][:, 0:2 * TS].rearrange("p (y n) -> p y n", y=2)).then_inc(t_dve, 1)
                elif kind == "qTs":
                    dve.wait_ge(t_done, t + 1)
                    for g in range(G):
                        for j in range(J):
                            ins = v.tensor_copy(q_bd[64 * g:64 * g + 64, :, (g * J + j) * TQ:(g * J + j + 1) * TQ],
                                                TB[t % 2][64 * g:64 * g + 64, j * TS:(j + 1) * TS].rearrange("p (b t) -> p b t", b=NB))
                    ins.then_inc(t_dve, 1)
                elif kind == "gates":
                    dve.wait_ge(gl_tanh, 1)
                    v.tensor_scalar(gate[:, 0:NT, :], gate[:, 0:NT, :], 0.5, 0.5, ALU.mult, ALU.add)
                    v.tensor_scalar(gate[0:TS, NT, :], gate[0:TS, NT, :], 0.5, 0.5, ALU.mult, ALU.add).then_inc(gate_ready, 1)
                    dve.wait_ge(gate_ready, 1)
                elif kind == "gr":
                    dve.wait_ge(t_done, t + 1)
                    for q in range(NQ):
                        seq(v.tensor_tensor(tmp[:, 0, 24 * q:24 * q + 24].rearrange("p (r h) -> p r h", r=3),
                                            TB[t % 2][:, 24 * q:24 * q + 24].rearrange("p (h r) -> p r h", r=3),
                                            cs("pick_head").unsqueeze(1).broadcast_to([P, 3, H]), ALU.mult))
                    v.tensor_reduce(gate_row[:, :, :], tmp[:, 0, 0:48].rearrange("p (q r h) -> p q r h", q=NQ, r=3), AX, ALU.add)\
                        .then_inc(t_dve, 1)
                elif kind == "ln":
                    i = s[1]
                    r = n_sp(i)
                    wait_main_read(dve, ("main", SLOT["V1"], i, 0))
                    seq(v.bn_stats(st[0:r, 100:106], vg[0:r, i, :]))
                    seq(v.bn_aggr(st[0:r, 106:108], st[0:r, 100:106]))
                    seq(v.tensor_copy(st[0:r, 15 + i:16 + i], st[0:r, 106:107]))
                    v.tensor_scalar(st[0:r, 20 + i:21 + i], st[0:r, 107:108], EPS, None, ALU.add).then_inc(var_ready, 1)
                elif kind == "ln2":
                    i = s[1]
                    if i == 0:
                        dve.wait_ge(std_ready, 1)
                        inverse_root(st[:, 25:30], st[:, 20:25], st[:, 120:125])
                    r = n_sp(i)
                    x = vg[0:r, i, :]
                    seq(v.scalar_tensor_tensor(x, x, st[0:r, 15 + i:16 + i], pm("v_g", r), ALU.subtract, ALU.mult))
                    v.scalar_tensor_tensor(x, x, st[0:r, 25 + i:26 + i], pm("v_b", r), ALU.mult, ALU.add).then_inc(vn_ready, 1)
                elif kind == "sp":
                    i = s[1]
                    dve.wait_ge(t_done, t + 1)
                    if i < NT:
                        v.tensor_tensor(sg[:, :, tok(i)], TB[t % 2][:, :].rearrange("p (g n) -> p g n", g=4),
                                        pm("b_sp").rearrange("p (g n) -> p g n", g=4), ALU.add).then_inc(t_dve, 1)
                    else:
                        for g in range(4):
                            ins = v.tensor_tensor(sg[:, g, TP:T].rearrange("p (b t) -> p b t", b=NB),
                                                  TB[t % 2][:, g * TS:(g + 1) * TS].rearrange("p (b t) -> p b t", b=NB),
                                                  pm("b_sp")[:, g * P:g * P + TQ].unsqueeze(1).broadcast_to([P, NB, TQ]), ALU.add)
                        ins.then_inc(t_dve, 1)
                elif kind == "main" and SLOTS[s[1]][0][0] in "UZ":
                    name, n, k = SLOTS[s[1]][0], MAIN_AT[s], FN_AT[s]
                    a, hf = s[2], s[3]
                    c = slice(hf * HALF, (hf + 1) * HALF)
                    f = tmp[:, k % 2, :]
                    if name[0] == "U":
                        wait_main_read(dve, s)
                        x = sg[:, 2 * int(name[1]) + a, c]
                        if k == 0:
                            wait_evacuated(dve, T_AT[("sp", NT)])
                        v.tensor_tensor(x, x, f, ALU.mult).then_inc(mix_fn, 1)
                    else:
                        dve.wait_ge(act_fn, k - 8 + 1)
                        tile = 2 * int(name[2]) + a
                        if name[1] == "A":
                            v.scalar_tensor_tensor(za[:, tile, c], f, 1.0, M[n % 2][:, 0:HALF], ALU.add, ALU.mult).then_inc(main_dve, 1)
                        else:
                            v.scalar_tensor_tensor(f, f, 1.0, M[n % 2][:, 0:HALF], ALU.add, ALU.mult).then_inc(main_dve, 1)
                            wait_main_read(dve, s)
                            v.scalar_tensor_tensor(sg[:, tile, c], sg[:, tile, c], 0.5, f, ALU.mult, ALU.mult).then_inc(mix_fn, 1)
                elif kind == "xt" and T_USE[t] == "dve":
                    c, n = s[1], s[2]
                    dve.wait_ge(t_done, t + 1)
                    if n == 0 and c:
                        dve.wait_ge(hid_sum, hid_count(c))
                    if c == 0 and n == 0:
                        dve.wait_ge(out_done, 16 * (N_OUT - 1))
                        dve.wait_ge(cmp_out, 32)
                    for dst, src in xt_parts(c, n, TB[t % 2]):
                        ins = v.tensor_copy(dst, src)
                    ins.then_inc(t_dve, 1)
                elif kind == "kc":
                    c = s[1]
                    dve.wait_ge(kc_done, c + 1)
                    if c < 3:
                        nb, nn = (QB, NCS) if c < 2 else (1, NCP)
                        for out, at, b2, tab in ((t1, 0, "b2k", "cos_blk"), (t2, 256, "b2kr", "sin_blk")):
                            seq(v.scalar_tensor_tensor(out[:, 0:nb * nn].rearrange("p (b n) -> p b n", b=nb),
                                                       S[2][:, at:at + nb * nn].rearrange("p (b n) -> p b n", b=nb), pm(b2),
                                                       cs(tab)[:, 0:nn].unsqueeze(1).broadcast_to([P, nb, nn]), ALU.add, ALU.mult))
                        if c < 2:
                            v.tensor_tensor(kcT[:, QB * c:QB * c + QB, :], t1.rearrange("p (b n) -> p b n", b=QB),
                                            t2.rearrange("p (b n) -> p b n", b=QB), ALU.add).then_inc(kc_ready, 1)
                        else:
                            for g in range(G):
                                r = slice(64 * g, 64 * g + 64)
                                ins = v.tensor_tensor(kcp[r, g, :], t1[r, 0:NCP], t2[r, 0:NCP], ALU.add)
                            ins.then_inc(kc_ready, 1)
                    elif c < 5:
                        v.tensor_tensor(vc[:, QB * (c - 3):QB * (c - 3) + QB, :], S[2][0:NCS, :].rearrange("p (b n) -> p b n", b=QB),
                                        pm("b2v", NCS).unsqueeze(1).broadcast_to([NCS, QB, P]), ALU.add).then_inc(kc_ready, 1)
                    else:
                        v.tensor_tensor(vcp[:, :], S[2][0:NCP, 0:P], pm("b2v", NCP), ALU.add).then_inc(kc_ready, 1)
                elif kind == "qkT":
                    b = s[1]
                    dve.wait_ge(t_done, t + 2)
                    if b:
                        dve.wait_ge(qk_done, b)
                    v.tensor_copy(kt_s[:, 512:1024], TB[(t + 1) % 2][:, :]).then_inc(t_dve, 1)
                elif kind == "s_max":
                    q = s[1]
                    dve.wait_ge(qk_done, QB * (q + 1))
                    seq(v.tensor_reduce(st[:, 30:31], O[:, 0:NCS], AX, ALU.max))
                    v.tensor_scalar(st[:, 31:32], st[:, 30:31], -SCALE, None, ALU.mult).then_inc(s_bias, 1)
                    dve.wait_ge(s_cexp, q + 1)
                    seq(v.reciprocal(st[:, 33:34], st[:, 32:33]))
                    v.tensor_scalar(ps[:, CMP:CMP + NCS], ps[:, CMP:CMP + NCS], st[:, 33:34], None, ALU.mult).then_inc(s_cp, 1)
                elif kind == "s_turn":
                    q = s[1]
                    dve.wait_ge(t_done, t + 1)
                    pj = pj_sum[0:NCS, 0:32]
                    v.tensor_reduce(pj.rearrange("p (b t) -> p b t", b=8),
                                    TB[t % 2][0:NCS, 0:P].rearrange("p (b j t) -> p b t j", b=8, j=J), AX, ALU.add).then_inc(t_dve, 1)
                    wait_evacuated(dve, t)
                    v.tensor_copy(pj_sum[0:NCS, 32:160].rearrange("p (b j t) -> p b j t", b=8, j=J),
                                  pj.rearrange("p (b t) -> p b t", b=8).unsqueeze(2).broadcast_to([NCS, 8, J, TQ])).then_inc(s_pj, 1)
                elif kind == "s_imp":
                    q = s[1]
                    dve.wait_ge(t_done, t + 1)
                    im = TB[t % 2][:, 1:15]
                    seq(v.tensor_reduce(st[:, 34:35], im, AX, ALU.min))
                    v.scalar_tensor_tensor(pick[:, 0:14], im, st[:, 34:35], cs("block_no"), ALU.is_le, ALU.mult).then_inc(t_dve, 1)
                    wait_evacuated(dve, t)
                    seq(v.tensor_reduce(st[:, 35:36], pick[:, 0:14], AX, ALU.max))
                    seq(v.tensor_scalar(st[:, 65:79], cs("block_no"), st[:, 35:36], NEG, ALU.is_equal, ALU.mult))
                    seq(v.tensor_copy(penalty.rearrange("p (n r) -> p n r", r=8), st[:, 64:80].unsqueeze(2).broadcast_to([P, 16, 8])))
                elif kind == "s_mask":
                    q = s[1]
                    nm = cs("new_mask")[:, q * TS:(q + 1) * TS]
                    for k in range(2):
                        v.tensor_tensor_reduce(ps[:, 512 * k:512 * k + 512].rearrange("p (s m) -> p s m", s=4),
                                               S[k][:, :].rearrange("p (s m) -> p s m", s=4),
                                               penalty.unsqueeze(1).broadcast_to([P, 4, P]), 1.0, -3e38, ALU.add, ALU.max,
                                               st[:, 40 + k:41 + k])
                    v.tensor_tensor_reduce(ps[:, 1024:1056], O[:, 64:96], nm, 1.0, -3e38, ALU.add, ALU.max, st[:, 42:43])
                    v.tensor_tensor_reduce(ps[:, WIN + 512:WIN + 544], O[:, 96:128], nm, 1.0, -3e38, ALU.add, ALU.max, st[:, 43:44])
                    early = S[2][:, 0:512:P]
                    seq(v.tensor_tensor(early, early, cs("win_mask"), ALU.add))
                    seq(v.tensor_reduce(st[:, 44:45], S[2][:, :], AX, ALU.max))
                    seq(v.tensor_reduce(st[:, 38:39], st[:, 40:43], AX, ALU.max))
                    seq(v.tensor_reduce(st[:, 39:40], st[:, 43:45], AX, ALU.max))
                    v.tensor_scalar(st[:, 46:48], st[:, 38:40], -SCALE, None, ALU.mult).then_inc(s_bias2, 1)
                elif kind == "s_scale":
                    q = s[1]
                    dve.wait_ge(s_exp, q + 1)
                    seq(v.tensor_tensor(st[:, 49:50], st[:, 49:50], st[:, 50:51], ALU.add))
                    seq(v.reciprocal(st[:, 36:38], st[:, 48:50]))
                    seq(v.tensor_tensor(st[:, 36:38], st[:, 36:38], gate_row[:, q, 1:3], ALU.mult))
                    v.tensor_scalar(ps[:, 0:1056], ps[:, 0:1056], st[:, 36:37], None, ALU.mult)
                    v.tensor_scalar(ps[:, WIN:WIN + 544], ps[:, WIN:WIN + 544], st[:, 37:38], None, ALU.mult)
                    v.tensor_scalar(ps[:, CMP:CMP + NCS], ps[:, CMP:CMP + NCS], gate_row[:, q, 0:1], None, ALU.mult).then_inc(s_p, 1)
                elif kind == "s_pv":
                    q = s[1]
                    dve.wait_ge(t_done, t + 1)
                    tb = TB[t % 2]
                    if q:
                        dve.wait_ge(o_done, q)
                    v.tensor_copy(pts[0:TS, 0:256], tb[0:TS, 0:256])
                    v.tensor_copy(pts[0:NCS, 256:384], tb[0:NCS, 256:384]).then_inc(t_dve, 1)
                    dve.wait_ge(t_done, t + 3)
                    v.tensor_copy(ptr[0], TB[(t + 2) % 2][:, :]).then_inc(t_dve, 1)
                elif kind == "s_out":
                    q = s[1]
                    dve.wait_ge(o_done, q + 1)
                    v.tensor_copy(o_row[:, :], O[:, 0:P]).then_inc(o_row_ready, 1)
                    dve.wait_ge(t_done, t + 1)
                    for g in range(G):
                        for j in range(J):
                            r = slice(64 * g, 64 * g + 64)
                            z = za[r, j, TP + 16 * q:TP + 16 * q + 16].rearrange("p (b t) -> p b t", b=QB)
                            o = TB[t % 2][r, 0:P].rearrange("p (b h t) -> p b h t", b=QB, h=H)[:, :, g * J + j, :]
                            ins = v.scalar_tensor_tensor(z, o, 0.5, z, ALU.mult, ALU.mult)
                    ins.then_inc(t_dve, 1)
                elif kind == "cs":
                    i = s[1]
                    dve.wait_ge(t_done, t + 1)
                    if i == 0:
                        dve.wait_ge(qk_done, NB)
                    else:
                        dve.wait_ge(t_done, T_AT[("ct", i - 1, 1)] + 1)
                    c3 = cp.rearrange("p (h n) -> p h n", h=H)
                    cm = cs("cmp_mask")[:, i * NCP:(i + 1) * NCP].unsqueeze(1).broadcast_to([P, H, NCP])
                    v.tensor_tensor(c3, TB[t % 2][:, 0:H * NCP].rearrange("p (h n) -> p h n", h=H), cm, ALU.add).then_inc(t_dve, 1)
                    wait_evacuated(dve, t)
                    seq(v.tensor_reduce(st[:, 0:8], c3, AX, ALU.max))
                    v.tensor_tensor(c3, c3, st[:, 0:8].unsqueeze(2).broadcast_to([P, H, NCP]), ALU.subtract).then_inc(c_in, 1)
                elif kind == "cn":
                    i = s[1]
                    c3 = cp.rearrange("p (h n) -> p h n", h=H)
                    dve.wait_ge(c_exp, i + 1)
                    seq(v.tensor_reduce(st[:, 8:16], c3, AX, ALU.add))
                    seq(v.reciprocal(st[:, 16:24], st[:, 8:16]))
                    gc = gate[:, i, :].rearrange("p (g j r) -> p j g r", g=G, j=J)[:, :, :, 0]
                    w = st[:, 16:24].rearrange("p (j g) -> p j g", j=J)
                    seq(v.tensor_tensor(w, w, gc, ALU.mult))
                    if i == 0:
                        seq(v.tensor_scalar(st[:, 16:24], st[:, 16:24], cs("row_mask"), None, ALU.mult))
                    v.tensor_tensor(c3, c3, st[:, 16:24].unsqueeze(2).broadcast_to([P, H, NCP]), ALU.mult).then_inc(c_p, 1)
                elif kind in ("ct", "pt") and t_uses(s) == ["dve"]:
                    dve.wait_ge(t_done, t + 1)
                    r = PT_AT[s]
                    if r >= NPT:
                        dve.wait_ge(pt_used, r - NPT + 1)
                    rows = NCP if kind == "ct" else P
                    v.tensor_copy(ptb[0:rows, r % NPT, :], TB[t % 2][0:rows, :]).then_inc(t_dve, 1)
                elif kind == "ps":
                    u = s[1]
                    i, g, y = UNITS[u]
                    n = (i + 1) * P
                    m = 80 + 20 * (u % 2)
                    if u < 2:
                        dve.wait_ge(o_done, NQ)
                    else:
                        dve.wait_ge(t_done, T_AT[("pt", u - 2, UNITS[u - 2][0])] + 1)
                    for j in range(J):
                        k = J * u + j
                        dve.wait_ge(p_scored, k + 1)
                        v.tensor_tensor_reduce(pb[:, u % 2, j, 0:n], S[k % 3][:, 0:n], cs("causal")[:, 512 - n:512], 1.0, -3e38,
                                               ALU.add, ALU.max, st[:, m + j:m + j + 1]).then_inc(p_masked, 1)
                    dve.wait_ge(p_masked, J * u + J)
                    v.tensor_scalar(st[:, m + 4:m + 8], st[:, m:m + 4], -SCALE, None, ALU.mult).then_inc(p_bias, 1)
                elif kind == "pn":
                    u = s[1]
                    i, g, y = UNITS[u]
                    n = (i + 1) * P
                    m = 80 + 20 * (u % 2)
                    dve.wait_ge(p_exp, u + 1)
                    seq(v.reciprocal(st[:, m + 12:m + 16], st[:, m + 8:m + 12]))
                    gy = gate[:, i, :].rearrange("p (g j r) -> p g j r", g=G, j=J)[:, g, :, y + 1]
                    seq(v.tensor_tensor(st[:, m + 12:m + 16], st[:, m + 12:m + 16], gy, ALU.mult))
                    for j in range(J):
                        ins = v.tensor_scalar(pb[:, u % 2, j, 0:n], pb[:, u % 2, j, 0:n], st[:, m + 12 + j:m + 13 + j], None, ALU.mult)
                    ins.then_inc(p_scaled, 1)
                elif kind == "oz":
                    i = s[1]
                    dve.wait_ge(pt_used, PT_AT[("pt", max(n for n, x in enumerate(UNITS) if x[0] == i), i)] + 1)
                    v.scalar_tensor_tensor(za[:, :, tok(i)], O[:, :].rearrange("p (j n) -> p j n", j=J), 0.5, za[:, :, tok(i)],
                                           ALU.mult, ALU.mult).then_inc(mix_ready, 1)
                elif kind == "zs":
                    k = s[1]
                    dve.wait_ge(x_split, k + 1)
                    v.tensor_tensor(x_lo[:, k, :], (za if k < 4 else sg)[:, k % 4, :], x_hi[:, k, :].bitcast(F32), ALU.subtract)\
                        .then_inc(x_lo_done, 1)
                elif kind == "main" and SLOTS[s[1]][1] == "wp":
                    _, sl, a_, hf, y = s
                    dt = 2 * (sl - SLOT["P0"]) + a_
                    c = slice(hf * HALF, (hf + 1) * HALF)
                    m = MAIN_AT[s]
                    dve.wait_ge(main_done, m + 1)
                    if dt == 0 and hf == 0 and y == 0:
                        wait_main_read(dve, ("main", SLOT["RB3"], 1, 1))
                    x = sig_at(y, dt)[:, c]
                    v.scalar_tensor_tensor(x, x, 1.0, M[m % 2][:, 0:HALF], ALU.add, ALU.mult).then_inc(main_dve, 1)
                    if y:
                        wait_main_read(dve, s)
                        a = sig_at(0, dt)[:, c]
                        v.tensor_tensor(a, a, x, ALU.add).then_inc(m_sum, 1)
                elif kind == "mlo":
                    _, dt, hf = s
                    c = slice(hf * HALF, (hf + 1) * HALF)
                    dve.wait_ge(m_hi, 2 * dt + hf + 1)
                    v.tensor_tensor(h_lo[:, dt, c], sig_at(0, dt)[:, c], h_hi[:, dt, c].bitcast(F32), ALU.subtract).then_inc(m_lo, 1)
                elif kind == "main" and SLOTS[s[1]][1] == "wo":
                    n, i, c = MAIN_AT[s], s[2], SLOTS[s[1]][2]
                    r = slice(0, P) if i < NT else slice(96, 128)
                    dve.wait_ge(main_done, n + 1)
                    if c == 0:
                        dve.wait_ge(xr_loaded[i], 16)
                    x = xr[i][r, c:c + 256]
                    v.scalar_tensor_tensor(x, M[n % 2][r, 0:256], 0.5, x, ALU.mult, ALU.add).then_inc(main_dve, 1)
                elif kind == "fin":
                    i = s[1]
                    k = LAST_TILES.index(i)
                    r = slice(0, P) if i < NT else slice(96, 128)
                    dve.wait_ge(f_ssq, 3 * len(LAST_TILES) + k + 1)
                    seq(v.tensor_reduce(st[r, i:i + 1], st[r, 20 + 4 * i:24 + 4 * i], AX, ALU.add))
                    v.tensor_scalar(st[r, 5 + i:6 + i], st[r, i:i + 1], 1.0 / D, EPS, ALU.mult, ALU.add).then_inc(f_ms, 1)
                    dve.wait_ge(f_root, k + 1)
                    inverse_root(st[r, 10 + i:11 + i], st[r, 5 + i:6 + i], st[r, 120:121])
                    if k == 0:
                        dve.wait_ge(fg_loaded, 16)
                    for n in range(2 if i == LAST_TILES[-1] else 1):
                        c = (slice(0, FIN_CUT), slice(FIN_CUT, D))[n]
                        v.scalar_tensor_tensor(xr[i][r, c], xr[i][r, c], st[r, 10 + i:11 + i], pm("norm_g")[r, c], ALU.mult, ALU.mult)\
                            .then_inc(f_out, 1)

        @block.tensor
        def _(pe):
            mm = nc.tensor.matmul

            def passes(out, lhs, rhs, n, before=None):
                for k in range(n):
                    if before:
                        before(k)
                    for a, b in ((0, 0), (0, 1), (1, 0)):
                        ins = mm(out, lhs(a, k), rhs(b, k), start=(k == 0 and a + b == 0), stop=(k == n - 1 and a == 1))
                return ins

            for s in ORDER:
                kind = s[0]
                t = T_AT[s]
                tb = TB[t % 2]
                if kind in ("xt",) or t_uses(s):
                    wait_t_bank(pe, t)
                if kind == "hT":
                    i = s[1]
                    n = n_sp(i)
                    pe.wait_ge(h_ready, i + 1)
                    if i == 0:
                        pe.wait_ge(ident_loaded, 16)
                    for hf in range(2):
                        if hf:
                            wait_t_bank(pe, t + hf)
                        for k in range(4):
                            kk = 4 * hf + k
                            ins = pe.transpose(TB[(t + hf) % 2][:, k * n:(k + 1) * n], xg[i][0:n, kk * P:(kk + 1) * P], ident[0:n, 0:n])
                        ins.then_inc(t_done, 1)
                elif kind == "wsT":
                    pe.wait_ge(ws_masked, 1)
                    for g in range(4):
                        ins = pe.transpose(tb[:, g * P:(g + 1) * P], ws_raw[:, g, :], ident)
                    ins.then_inc(t_done, 1)
                elif kind == "wbd":
                    wait_evacuated(pe, T_AT[("wsT",)])
                    pe.wait_ge(const_loaded, 32)
                    mm(tb[0:TS, 0:16].rearrange("p (g t) -> p g t", g=4), cs("repeat4", TQ), wsT[0:TQ, :, 0:TQ], start=True, stop=True)\
                        .then_inc(t_done, 1)
                elif kind == "kT":
                    pe.wait_ge(rope_step, ROPE_STEPS[s[1]])
                    for i in range(NT):
                        ins = pe.transpose(tb[:, tok(i)], kq[:, i, 128 * s[1]:128 * s[1] + 128], ident)
                    ins.then_inc(t_done, 1)
                elif kind == "kTs":
                    for y in range(2):
                        ins = pe.transpose(tb[:, y * TS:(y + 1) * TS], kq[0:TS, NT, 128 * y:128 * y + 128], ident[0:TS, 0:TS])
                    ins.then_inc(t_done, 1)
                elif kind in ("qT", "qTs"):
                    i = s[1] if kind == "qT" else NT
                    n = n_sp(i)
                    pe.wait_ge(rope_step, ROPE_STEPS[2])
                    for j in range(J):
                        src = kq[0:n, i, 512 + j * P:512 + (j + 1) * P]
                        ins = pe.transpose(tb[:, j * n:(j + 1) * n], src, ident[0:n, 0:n])
                    ins.then_inc(t_done, 1)
                elif kind == "gr":
                    pe.wait_ge(gate_ready, 1)
                    for q in range(NQ):
                        ins = mm(tb[:, 24 * q:24 * q + 24], cs("pick_rows", TS)[:, q * P:(q + 1) * P], gate[0:TS, NT, :], start=True, stop=True)
                    ins.then_inc(t_done, 1)
                elif kind == "main":
                    n = MAIN_AT[s]
                    wait_main_bank(pe, n)
                    out = M[n % 2]
                    sl = s[1]
                    name, mk, _, w = SLOTS[sl]
                    if MAIN_AT[s]:
                        pe.wait_ge(lo_done, 2 * sl + 2)
                    hx, wx = (h_hi, h_lo), (w_hi, w_lo)
                    if mk in ("tm", "wo"):
                        i = s[2]
                        if sl == 0:
                            wait_evacuated(pe, T_AT[("hT", i)] + 1)
                        before = (lambda k: pe.wait_ge(m_lo, 2 * k + 2)) if s == ("main", SLOT["WO0"], LAST_TILES[0], 0) else None
                        if n == 0:
                            before = lambda k: pe.wait_ge(lo_done, 1 + k // 4)
                        c = tok(i) if i < NT else slice(T - P, T)
                        ins = passes(out[:, 0:w], lambda a, k: hx[a][:, k, c], lambda b, k: wx[b][:, sl % 2, k, 0:w], KD, before)
                    elif mk == "wp":
                        _, _, a_, hf, y = s
                        if sl == SLOT["P0"] and a_ == 0 and hf == 0:
                            pe.wait_ge(x_lo_done, 4 + 4 * y)
                        xx = (x_hi, x_lo)
                        ins = passes(out[:, 0:HALF], lambda a, k: wx[a][:, sl % 2, 4 * y + k, a_ * P:(a_ + 1) * P],
                                     lambda b, k: xx[b][:, 4 * y + k, hf * HALF:(hf + 1) * HALF], 4)
                    else:
                        a_, hf = s[2], s[3]
                        lhs = lambda a, k: wx[a][:, sl % 2, k, a_ * P:(a_ + 1) * P]
                        ins = passes(out[:, 0:HALF], lhs, lambda b, k: hx[b][:, k, hf * HALF:(hf + 1) * HALF], KD)
                    ins.then_inc(main_done, 1)
                elif kind == "sp":
                    i = s[1]
                    n = n_sp(i)
                    pe.wait_ge(vn_ready, i + 1)
                    if i == NT:
                        wait_evacuated(pe, T_AT[("wbd",)])
                    for g in range(4):
                        w = wsT[:, g, :] if i < NT else w_bd[:, g, :]
                        ins = mm(tb[:, g * n:(g + 1) * n], vg[0:n, i, g * P:(g + 1) * P], w, start=True, stop=True)
                    ins.then_inc(t_done, 1)
                elif kind == "xt":
                    c, n = s[1], s[2]
                    w, cc = part(c)
                    b, r = divmod(n, 2)
                    ld = LOAD_AT[(w, "p" if cc == 2 else cc * QB + b)]
                    pe.wait_ge(ring_loaded[ld % RING], 16 * (ld // RING + 1))
                    x = ring[:, ld % RING, :]
                    if cc < 2:
                        for q in range(4):
                            ins = pe.transpose(tb[:, q * P:(q + 1) * P], x[:, (2 * q + r) * P:(2 * q + r + 1) * P], ident)
                    else:
                        for k in range(8):
                            r, q = divmod(k, 4)
                            ins = pe.transpose(tb[:, k * 64:k * 64 + 64], x[0:64, (2 * q + r) * P:(2 * q + r + 1) * P], ident[0:64, 0:64])
                    ins.then_inc(t_done, 1)
                elif kind == "hid":
                    c = s[1]
                    w, cc = part(c)
                    w1 = w1_at[c // 3]
                    pe.wait_ge(w1_loaded[c // 3], 16)
                    for k in range(8 if cc < 2 else 1):
                        if k >= (6 if cc < 2 else 0):
                            wait_evacuated(pe, T_AT[("xt", c, k)])
                    if c:
                        pe.wait_ge(hid_ready, hid_count(c))
                    for g in range(G if cc < 2 else 1):
                        for j in range(16):
                            o = j // 4
                            if cc < 2:
                                rhs = xt[:, j % 4, g, :].rearrange("p (b m) -> p b m", b=QB)[:, :, o:o + 2 * NCS - 1:2]
                                out = S[g][:, 0:252]
                            else:
                                rhs = xtp[:, j % 4, :, o:o + 2 * NCP - 1:2]
                                out = S[0][:, 0:2 * NCP]
                            ins = mm(out, w1[:, j, :], rhs, start=(j == 0), stop=(j == 15))
                        ins.then_inc(hid_sum, 1)
                elif kind == "kc":
                    c = s[1]
                    pe.wait_ge(hid_ready, hid_count(c + 1))
                    if c:
                        pe.wait_ge(kc_ready, c)
                    if c < 3:
                        n = 252 if c < 2 else NCP
                        for g in range(G):
                            x = hid[:, g, :] if c < 2 else hid[:, 0, g * NCP:(g + 1) * NCP]
                            for k, w2 in enumerate(("w2k", "w2kr")):
                                ins = mm(S[2][64 * g:64 * g + 64, 256 * k:256 * k + n], pm(w2), x, start=True, stop=True)
                    elif c < 5:
                        for b in range(QB):
                            for g in range(G):
                                ins = mm(S[2][0:NCS, b * P + g * DH:b * P + (g + 1) * DH], hid[:, g, b * NCS:(b + 1) * NCS], pm("w2v"),
                                         start=True, stop=True)
                    else:
                        for g in range(G):
                            ins = mm(S[2][0:NCP, g * DH:(g + 1) * DH], hid[:, 0, g * NCP:(g + 1) * NCP], pm("w2v"), start=True, stop=True)
                    ins.then_inc(kc_done, 1)
                elif kind == "qkT":
                    b = s[1]
                    for k in range(3):
                        ld = LOAD_AT[("ks" if k < 2 else "kw", b)]
                        if k != 1:
                            pe.wait_ge(ring_loaded[ld % RING], 16 * (ld // RING + 1))
                        if k:
                            wait_t_bank(pe, t + k)
                        for q in range(4):
                            x = ring[:, ld % RING, (4 * (k % 2) + q) * P:(4 * (k % 2) + q + 1) * P]
                            ins = pe.transpose(TB[(t + k) % 2][:, q * P:(q + 1) * P], x, ident)
                        ins.then_inc(t_done, 1)
                elif kind == "qkS":
                    b = s[1]
                    for k in range(3):
                        wait_evacuated(pe, T_AT[("qkT", b)] + k)
                    if b == 0:
                        pe.wait_ge(kc_ready, 6)
                        wait_evacuated(pe, T_AT[("qTs",)])
                        wait_evacuated(pe, T_AT[("kTs",)])
                    if b == QB:
                        pe.wait_ge(s_exp, 1)
                        pe.wait_ge(o_row_ready, 1)
                    r = slice(32 * (b % QB), 32 * (b % QB) + 32)
                    q = q_bd[:, b, :]
                    for k in range(2):
                        mm(S[k][r, :], q, kt_s[:, 512 * k:512 * k + 512], start=True, stop=True)
                    mm(S[2][r, :], q, kt_w, start=True, stop=True)
                    mm(O[r, 0:NCS], q, kcT[:, b, :], start=True, stop=True)
                    for y in range(2):
                        ins = mm(O[r, 64 + 32 * y:96 + 32 * y], q, k_newT[:, y, :], start=True, stop=True)
                    ins.then_inc(qk_done, 1)
                elif kind == "s_turn":
                    pe.wait_ge(s_cp, s[1] + 1)
                    pe.transpose(tb[0:NCS, 0:P], ps[:, CMP:CMP + NCS], ident).then_inc(t_done, 1)
                elif kind == "s_imp":
                    pe.wait_ge(s_pj, s[1] + 1)
                    mm(tb[:, 0:NSEL], pj_sum[0:NCS, 32:160], cs("overlap", NCS), start=True, stop=True).then_inc(t_done, 1)
                elif kind == "s_pv":
                    q = s[1]
                    pe.wait_ge(s_p, q + 1)
                    pe.transpose(tb[0:TS, 0:P], ps[:, 1024:1056], ident)
                    pe.transpose(tb[0:TS, P:2 * P], ps[:, WIN + 512:WIN + 544], ident)
                    pe.transpose(tb[0:NCS, 2 * P:3 * P], ps[:, CMP:CMP + NCS], ident).then_inc(t_done, 1)

                    def turn(k):
                        c0 = (0, 0, 512, WIN)[k]
                        wait_t_bank(pe, t + k)
                        for m in range(4):
                            ins = pe.transpose(TB[(t + k) % 2][:, m * P:(m + 1) * P], ps[:, c0 + m * P:c0 + (m + 1) * P], ident)
                        ins.then_inc(t_done, 1)

                    turn(1)
                    wait_evacuated(pe, t)
                    pe.wait_ge(v_loaded, 16 * 2 * QB * (q + 1))
                    for y in range(2):
                        mm(O[:, 0:P], pts[0:TS, y * P:(y + 1) * P], v_tok[0:TS, y, NT, :], start=(y == 0), stop=False, skip_group_check=True)
                    for b in range(QB):
                        mm(O[32 * b:32 * b + 32, 0:P], pts[0:NCS, 2 * P + 32 * b:2 * P + 32 * b + 32], vc[:, QB * q + b, :],
                           start=False, stop=False, skip_group_check=True)
                    for k in range(1, 4):
                        if k < 3:
                            turn(k + 1)
                        wait_evacuated(pe, t + k)
                        src = (None, ptr[1], ptr[0], ptr[1])[k]
                        for b in range(QB):
                            for m in range(4):
                                val = vs[:, b, 4 * (k - 1) + m, :] if k < 3 else vw[:, b, m, :]
                                ins = mm(O[32 * b:32 * b + 32, 0:P], src[:, m * P + 32 * b:m * P + 32 * b + 32], val,
                                         start=False, stop=(k == 3 and m == 3), skip_group_check=True)
                        ins.then_inc(pv_part if k < 3 else o_done, 1)
                elif kind == "s_out":
                    pe.wait_ge(o_row_ready, s[1] + 1)
                    pe.transpose(tb[:, 0:P], o_row[:, :], ident).then_inc(t_done, 1)
                elif kind == "cs":
                    i = s[1]
                    if i == 0:
                        wait_evacuated(pe, T_AT[("qT", NT - 1)])
                        wait_evacuated(pe, T_AT[("kT", 1)])
                    for j in range(J):
                        ins = mm(tb[:, j * 2 * NCP:(j + 1) * 2 * NCP].rearrange("p (g n) -> p g n", g=G), qT[:, j, tok(i)], kcp[:, :, :], start=True, stop=True)
                    ins.then_inc(t_done, 1)
                elif kind == "ct":
                    i, g = s[1], s[2]
                    pe.wait_ge(c_p, i + 1)
                    for j in range(J):
                        c0 = (j * G + g) * NCP
                        ins = pe.transpose(tb[0:NCP, j * P:(j + 1) * P], cp[:, c0:c0 + NCP], ident)
                    ins.then_inc(t_done, 1)
                elif kind == "cv":
                    i, g = s[1], s[2]
                    if g == 0 and i:
                        pe.wait_ge(mix_ready, i)
                    wait_evacuated(pe, T_AT[("ct", i, g)])
                    mm(O[64 * g:64 * g + 64, :], vcp[:, g * DH:(g + 1) * DH], ptb[0:NCP, PT_AT[("ct", i, g)] % NPT, :], start=True, stop=False,
                       skip_group_check=True).then_inc(pt_used, 1)
                elif kind == "ps":
                    u = s[1]
                    i, g, y = UNITS[u]
                    n = (i + 1) * P
                    for j in range(J):
                        k = J * u + j
                        if k >= 3:
                            pe.wait_ge(p_masked, k - 2)
                        if k == 0:
                            pe.wait_ge(s_exp, NQ)
                        mm(S[k % 3][:, 0:n], qT[:, j, tok(i)], k_pad[:, y, g, 0:n], start=True, stop=True).then_inc(p_scored, 1)
                elif kind == "pt":
                    u, kt = s[1], s[2]
                    i, g, y = UNITS[u]
                    if kt == 0:
                        pe.wait_ge(p_scaled, u + 1)
                    for j in range(J):
                        ins = pe.transpose(tb[:, j * P:(j + 1) * P], pb[:, u % 2, j, kt * P:(kt + 1) * P], ident)
                    ins.then_inc(t_done, 1)
                elif kind == "pp":
                    u, k = s[1], s[2]
                    i, g, y = UNITS[u]
                    wait_evacuated(pe, T_AT[("pt", u, k)])
                    mm(O[64 * g:64 * g + 64, :], v_tok[:, y, k, g * DH:(g + 1) * DH], ptb[:, PT_AT[("pt", u, k)] % NPT, :],
                       start=False, stop=(y == 1 and k == i), skip_group_check=True).then_inc(pt_used, 1)


OUTS = [("y_p", (TP, D)), ("y_s", (TS, D)), ("pk_cmp", (TP, P)), ("pv_cmp", (TP, P)), ("pk_sel", (TP, P)),
        ("pv_sel", (TP, P)), ("pk_win", (TP, P)), ("pv_win", (TP, P)), ("sk_cmp", (TS, P)), ("sv_cmp", (TS, P)),
        ("sk_sel", (TS, P)), ("sv_sel", (TS, P)), ("sk_win", (NB, 512, P)), ("sv_win", (NB, 512, P)), ("s_chunk", (TS, 512))]


def kernel(x_prompt, x_sample, cache_k_cmp, cache_v_cmp, cache_k_sel, cache_v_sel, cache_k_win, cache_v_win, page_table,
           norm_g, w_in, cmp_k_w1, cmp_k_b1, cmp_k_w2, cmp_k_b2, cmp_v_w1, cmp_v_b1, cmp_v_w2, cmp_v_b2,
           v_norm_g, v_norm_b, w_spatial, b_spatial, w_pa, w_pb, w_o, final_g):
    import concourse.bacc as bacc
    from concourse.bass_utils import run_bass_kernel_spmd

    A = np.asarray

    def rows(a, n=P):
        return np.ascontiguousarray(np.broadcast_to(A(a).reshape(1, -1), (n, A(a).size)))

    def turned(a):
        return np.concatenate([a[..., 8:16], a[..., 0:8], a[..., 16:]], -1)

    def column(a):
        return np.tile(A(a).reshape(-1, 1), (P // A(a).size, 1))

    params = np.zeros((P, N_PARAM), np.float32)
    for name, a in (("norm_g", rows(norm_g)), ("v_g", rows(v_norm_g)), ("v_b", rows(v_norm_b)), ("b_sp", rows(b_spatial)),
                    ("w2k", A(cmp_k_w2)[0]), ("w2kr", turned(A(cmp_k_w2)[0])), ("w2v", A(cmp_v_w2)[0]),
                    ("b1k", column(cmp_k_b1)), ("b1v", column(cmp_v_b1)), ("b2k", column(cmp_k_b2)),
                    ("b2kr", column(turned(A(cmp_k_b2)[0]))), ("b2v", rows(np.concatenate([A(cmp_v_b2)[0]] * 2)))):
        params[:, PARAMS[name][0]:PARAMS[name][1]] = a
    given = [
        ("x_p", A(x_prompt).reshape(TP, D)), ("x_s", A(x_sample).reshape(TS, D)),
        ("ck_cmp", A(cache_k_cmp).reshape(-1, 8 * P)), ("cv_cmp", A(cache_v_cmp).reshape(-1, 8 * P)),
        ("ck_sel", A(cache_k_sel).reshape(-1, 8 * P)), ("cv_sel", A(cache_v_sel).reshape(-1, 8 * P)),
        ("ck_win", A(cache_k_win).reshape(NB, 512, P)), ("cv_win", A(cache_v_win).reshape(NB, 512, P)),
        ("pages", np.repeat(A(page_table).T, P // (PAST // PAGE), axis=0)),
        ("w_in", A(w_in)[0]), ("w1k", A(cmp_k_w1)[0]), ("w1v", A(cmp_v_w1)[0]), ("w_sp", A(w_spatial)[0].transpose(1, 0, 2)),
        ("w_pa", A(w_pa)[0]), ("w_pb", A(w_pb)[0]), ("w_o", A(w_o)[0]), ("final_g", rows(final_g)),
        ("params", params), ("consts", constants()),
    ]
    nc = bacc.Bacc("TRN2", target_bir_lowering=False, num_devices=1)
    arrays, args = {}, []
    for name, a in given:
        a = np.ascontiguousarray(a)
        arrays["in_" + name] = a
        args.append(nc.dram_tensor("in_" + name, a.shape, mybir.dt.from_np(a.dtype), kind="ExternalInput").ap())
    outs = [nc.dram_tensor("out_" + name, shape, F32, kind="ExternalOutput").ap() for name, shape in OUTS]
    nsa_gmlp_layer(nc, *args, outs)
    r = run_bass_kernel_spmd(nc, [arrays], core_ids=[0]).results[0]
    got = {name: r["out_" + name] for name, _ in OUTS}
    heads = (G, DH)
    return (got["y_p"].reshape(1, TP, D), got["y_s"].reshape(NB, TQ, D),
            *(got[n].reshape(1, 1, TP, *heads) for n in ("pk_cmp", "pv_cmp", "pk_sel", "pv_sel", "pk_win", "pv_win")),
            *(got[n].reshape(1, NB, TQ, *heads) for n in ("sk_cmp", "sv_cmp", "sk_sel", "sv_sel")),
            *(got[n].reshape(1, NB, 512, *heads) for n in ("sk_win", "sv_win")),
            got["s_chunk"].reshape(1, NB, TQ, 512))
```
